# Optimizing a Trainium2 kernel written in Bass

```python
import jax
import jax.numpy as jnp
from jax import lax
import numpy as np

D_MODEL = 1024
BATCH = 1
SEQ = 512
DEPTH = 2

RET_HEADS = 4
RET_DK = 128
RET_DV = 256
RET_CHUNK = 128
SWA_Q_HEADS = 16
SWA_KV_HEADS = 2
SWA_HEAD_DIM = 64
WINDOW = 128
SWA_BLOCK = 128
D_FF = 2816
ROPE_THETA = 10000.0
NORM_EPS = 1e-6
MAX_POS_OFFSET = 1024
N_MOD = 9

RET_QK_WIDTH = RET_HEADS * RET_DK
RET_V_WIDTH = RET_HEADS * RET_DV
SWA_Q_WIDTH = SWA_Q_HEADS * SWA_HEAD_DIM
SWA_KV_WIDTH = SWA_KV_HEADS * SWA_HEAD_DIM
IN_SPLITS = (RET_QK_WIDTH, RET_QK_WIDTH, RET_V_WIDTH, RET_V_WIDTH, SWA_Q_WIDTH, SWA_KV_WIDTH, SWA_KV_WIDTH, D_MODEL, D_MODEL)
IN_COLS = sum(IN_SPLITS)

kernel_name = 'hybrid_retention_swa_macaron_adaln'

def rmsnorm(x, gain):
    xf = x.astype(jnp.float32)
    y = xf * lax.rsqrt(jnp.mean(xf * xf, axis=-1, keepdims=True) + NORM_EPS)
    return (y * gain.astype(jnp.float32)).astype(x.dtype)

def modulate(h, shift, scale):
    return h * (1 + scale[:, None, :]) + shift[:, None, :]

def swiglu(h, w_up, w_down):
    gate, up = jnp.split(h @ w_up, 2, axis=-1)
    return (jax.nn.silu(gate) * up) @ w_down

def rope_tables(positions, dim):
    inv_freq = 1.0 / (ROPE_THETA ** (jnp.arange(0, dim, 2, dtype=jnp.float32) / dim))
    ang = positions.astype(jnp.float32)[..., None] * inv_freq
    return jnp.cos(ang), jnp.sin(ang)

def apply_rope(x, cos, sin):
    xf = x.astype(jnp.float32)
    x1, x2 = jnp.split(xf, 2, axis=-1)
    c = cos[:, :, None, :]
    s = sin[:, :, None, :]
    return jnp.concatenate([x1 * c - x2 * s, x2 * c + x1 * s], axis=-1).astype(x.dtype)

def head_groupnorm(y):
    mu = jnp.mean(y, axis=-1, keepdims=True)
    var = jnp.mean(jnp.square(y - mu), axis=-1, keepdims=True)
    return (y - mu) * lax.rsqrt(var + NORM_EPS)

def chunkwise_retention(q, k, v):
    B, T, H, dk = q.shape
    dv = v.shape[-1]
    C = RET_CHUNK
    N = T // C
    f32 = jnp.float32
    log_gamma = jnp.log1p(-(2.0 ** (-5.0 - jnp.arange(H, dtype=f32))))
    qc = (q.astype(f32) * (dk ** -0.5)).reshape(B, N, C, H, dk)
    kc = k.astype(f32).reshape(B, N, C, H, dk)
    vc = v.astype(f32).reshape(B, N, C, H, dv)
    idx = jnp.arange(C, dtype=f32)
    rel = idx[:, None] - idx[None, :]
    decay_intra = jnp.where(rel[None] >= 0,
                            jnp.exp(jnp.maximum(rel, 0.0)[None] * log_gamma[:, None, None]),
                            0.0)
    scores = jnp.einsum('bnihd,bnjhd->bnhij', qc, kc) * decay_intra[None, None]
    intra = jnp.einsum('bnhij,bnjhe->bnihe', scores, vc)
    zeta = jnp.exp((C - 1 - idx)[None, :] * log_gamma[:, None])
    xi = jnp.exp((idx + 1)[None, :] * log_gamma[:, None])
    chunk_kv = jnp.einsum('bnjhd,hj,bnjhe->nbhde', kc, zeta, vc)
    gamma_chunk = jnp.exp(C * log_gamma)[None, :, None, None]

    def step(state, kv_n):
        return state * gamma_chunk + kv_n, state

    _, prev_states = lax.scan(step, jnp.zeros((B, H, dk, dv), f32), chunk_kv)
    cross = jnp.einsum('bnihd,nbhde,hi->bnihe', qc, prev_states, xi)
    return (intra + cross).reshape(B, T, H, dv)

def sliding_window_gqa_sinks(q, k, v, sinks):
    B, T, Hq, d = q.shape
    Hkv = k.shape[2]
    G = Hq // Hkv
    C = SWA_BLOCK
    N = T // C
    qb = q.reshape(B, N, C, Hkv, G, d)
    kb = k.reshape(B, N, C, Hkv, d)
    vb = v.reshape(B, N, C, Hkv, d)
    pad = jnp.zeros_like(kb[:, :1])
    k2 = jnp.concatenate([jnp.concatenate([pad, kb[:, :-1]], axis=1), kb], axis=2)
    v2 = jnp.concatenate([jnp.concatenate([pad, vb[:, :-1]], axis=1), vb], axis=2)
    scores = jnp.einsum('bnikgd,bnjkd->bkgnij', qb, k2).astype(jnp.float32) * (d ** -0.5)
    qi = jnp.arange(C)[:, None] + C
    kj = jnp.arange(2 * C)[None, :]
    rel = qi - kj
    band = (rel >= 0) & (rel < WINDOW)
    blk_valid = (jnp.arange(N)[:, None, None] > 0) | (kj >= C)[None]
    mask = band[None] & blk_valid
    scores = jnp.where(mask, scores, -jnp.inf)
    sink = jnp.broadcast_to(sinks.astype(jnp.float32).reshape(Hkv, G)[None, :, :, None, None, None],
                            scores.shape[:-1] + (1,))
    logits = jnp.concatenate([scores, sink], axis=-1)
    m = jnp.max(logits, axis=-1, keepdims=True)
    p = jnp.exp(logits - m)
    probs = p[..., :-1] / jnp.sum(p, axis=-1, keepdims=True)
    out = jnp.einsum('bkgnij,bnjkd->bnikgd', probs.astype(v.dtype), v2)
    return out.reshape(B, T, Hq * d)

def hybrid_mixer(h, cos_r, sin_r, cos_s, sin_s, w_in, sinks, w_branch_ret, w_branch_swa, w_out):
    B, T, _ = h.shape
    offsets = np.cumsum(IN_SPLITS)[:-1]
    rq, rk, rv, rg, sq, sk, sv, gate_r, gate_s = jnp.split(h @ w_in, offsets, axis=-1)
    rq = apply_rope(rq.reshape(B, T, RET_HEADS, RET_DK), cos_r, sin_r)
    rk = apply_rope(rk.reshape(B, T, RET_HEADS, RET_DK), cos_r, sin_r)
    ret = chunkwise_retention(rq, rk, rv.reshape(B, T, RET_HEADS, RET_DV))
    ret = head_groupnorm(ret).reshape(B, T, RET_V_WIDTH).astype(h.dtype)
    ret = jax.nn.silu(rg) * ret
    branch_ret = ret @ w_branch_ret
    sq = apply_rope(sq.reshape(B, T, SWA_Q_HEADS, SWA_HEAD_DIM), cos_s, sin_s)
    sk = apply_rope(sk.reshape(B, T, SWA_KV_HEADS, SWA_HEAD_DIM), cos_s, sin_s)
    sv = sv.reshape(B, T, SWA_KV_HEADS, SWA_HEAD_DIM)
    branch_swa = sliding_window_gqa_sinks(sq, sk, sv, sinks) @ w_branch_swa
    merged = jax.nn.sigmoid(gate_r) * branch_ret + jax.nn.sigmoid(gate_s) * branch_swa
    return merged @ w_out

def setup_inputs(seed: int = 0) -> dict:
    key = jax.random.key(seed)
    ks = jax.random.split(key, 20)
    f32 = jnp.float32

    def dense(k, shape, fan_in, mult=1.0):
        return jax.random.normal(k, shape, f32) * (mult * fan_in ** -0.5)

    def gains(k, shape):
        return 1.0 + 0.05 * jax.random.normal(k, shape, f32)

    x = jax.random.normal(ks[0], (BATCH, SEQ, D_MODEL), f32)
    c = jax.random.normal(ks[1], (BATCH, D_MODEL), f32)
    offset = jax.random.randint(ks[2], (BATCH, 1), 0, MAX_POS_OFFSET, dtype=jnp.int32)
    positions = (offset + jnp.arange(SEQ, dtype=jnp.int32)[None, :]).astype(jnp.int32)
    return {
        'x': x,
        'c': c,
        'positions': positions,
        'norm_ffn1': gains(ks[3], (DEPTH, D_MODEL)),
        'norm_mix': gains(ks[4], (DEPTH, D_MODEL)),
        'norm_ffn2': gains(ks[5], (DEPTH, D_MODEL)),
        'final_norm': gains(ks[6], (D_MODEL,)),
        'w_ada': dense(ks[7], (DEPTH, D_MODEL, N_MOD * D_MODEL), D_MODEL, 0.5),
        'b_ada': 0.02 * jax.random.normal(ks[8], (DEPTH, N_MOD * D_MODEL), f32),
        'ffn1_w_up': dense(ks[9], (DEPTH, D_MODEL, 2 * D_FF), D_MODEL),
        'ffn1_w_down': dense(ks[10], (DEPTH, D_FF, D_MODEL), D_FF),
        'ffn2_w_up': dense(ks[11], (DEPTH, D_MODEL, 2 * D_FF), D_MODEL),
        'ffn2_w_down': dense(ks[12], (DEPTH, D_FF, D_MODEL), D_FF),
        'w_in': dense(ks[13], (DEPTH, D_MODEL, IN_COLS), D_MODEL),
        'sinks': jax.random.normal(ks[14], (DEPTH, SWA_Q_HEADS), f32),
        'w_branch_ret': dense(ks[15], (DEPTH, RET_V_WIDTH, D_MODEL), RET_V_WIDTH),
        'w_branch_swa': dense(ks[16], (DEPTH, SWA_Q_WIDTH, D_MODEL), SWA_Q_WIDTH),
        'w_out': dense(ks[17], (DEPTH, D_MODEL, D_MODEL), D_MODEL),
    }

def reference(x, c, positions, norm_ffn1, norm_mix, norm_ffn2, final_norm, w_ada, b_ada,
              ffn1_w_up, ffn1_w_down, ffn2_w_up, ffn2_w_down, w_in, sinks,
              w_branch_ret, w_branch_swa, w_out):
    cos_r, sin_r = rope_tables(positions, RET_DK)
    cos_s, sin_s = rope_tables(positions, SWA_HEAD_DIM)
    c_act = jax.nn.silu(c)
    for l in range(DEPTH):
        mod = c_act @ w_ada[l] + b_ada[l]
        sh1, sc1, g1, sh2, sc2, g2, sh3, sc3, g3 = jnp.split(mod, N_MOD, axis=-1)
        h = modulate(rmsnorm(x, norm_ffn1[l]), sh1, sc1)
        x = x + 0.5 * g1[:, None, :] * swiglu(h, ffn1_w_up[l], ffn1_w_down[l])
        h = modulate(rmsnorm(x, norm_mix[l]), sh2, sc2)
        x = x + g2[:, None, :] * hybrid_mixer(h, cos_r, sin_r, cos_s, sin_s, w_in[l], sinks[l],
                                              w_branch_ret[l], w_branch_swa[l], w_out[l])
        h = modulate(rmsnorm(x, norm_ffn2[l]), sh3, sc3)
        x = x + 0.5 * g3[:, None, :] * swiglu(h, ffn2_w_up[l], ffn2_w_down[l])
    return rmsnorm(x, final_norm)


_drawn_inputs = setup_inputs


def setup_inputs(seed=0):
    import zlib

    import numpy as np

    out = dict(_drawn_inputs(seed))
    spreads = {}
    factors = {'norm_ffn1': 5.276, 'norm_mix': 3.673, 'norm_ffn2': 5.129, 'sinks': 38.052}
    for name, (base, spread) in spreads.items():
        noise = np.random.default_rng([zlib.crc32(name.encode()), seed]).standard_normal(out[name].shape)
        drawn = base * np.exp(spread * noise) if base else spread * noise
        out[name] = jnp.asarray(drawn.astype(out[name].dtype))
    for name, factor in factors.items():
        out[name] = (out[name] * factor).astype(out[name].dtype)
    return out
```

```python
import numpy as np

import concourse.bass as bass
from concourse import mybir
from contextlib import ExitStack, contextmanager

D, T, DEPTH, P = 1024, 512, 2, 128
FF = 2816
KT = D // P
TT = T // P
FT = FF // P
HALF = FT // 2
RH, DV = 4, 256
QH, HD = 16, 64
EPS = 1e-6
MOD_TILES = 9 * KT
RQ, RK, RG, SQ, SK, SV, GR, GS = 0, 4, 16, 24, 32, 33, 34, 42
RV_COL = 1024
UP_UNIT, DOWN_UNIT = KT * P, HALF * P

HALF_PAIRS = HALF + KT // 2
FFN_PAIRS = 2 * HALF_PAIRS
V_PAIRS = 4
MIX0 = FFN_PAIRS
KV_PAIR = MIX0 + V_PAIRS
HEAD0 = KV_PAIR + 1
GATE_S0 = HEAD0 + 3 * RH
GATE_R0 = GATE_S0 + KT
OUT0 = GATE_R0 + KT
FFN2 = OUT0 + KT // 2
LAYER_PAIRS = FFN2 + FFN_PAIRS
UNGATED = V_PAIRS + 1
LAYER_GATED = LAYER_PAIRS - UNGATED
JOBS, FIRST_JOBS = 36, 8
HALF_JOBS = (JOBS - FIRST_JOBS) // 2
LAYER_SPLITS = 4 * KT
LAYER_ROPES = 1 + 4 * RH
LAYER_STEPS = 157
TWO_PI = 6.283185307179586
C1 = 6.28125
C2 = float(np.float32(TWO_PI - C1).view(np.uint32) & 0xFFFFF000)
C2 = float(np.array(int(C2), np.uint32).view(np.float32))
C3 = float(np.float32(TWO_PI - C1 - C2))
ROUND = 12582912.0
MASKED = -1e30

K_ID, K_COL = 0, P
K_DECAY = K_COL + 8
K_MASK = K_DECAY + RH * T
K_ALL = K_MASK + 2 * T


def constants():
    k = np.zeros((P, K_ALL), np.float32)
    k[:, K_ID:K_ID + P] = np.eye(P, dtype=np.float32)
    p = np.arange(P)
    for col, half in ((0, 64), (2, 32)):
        freq = (np.float32(1.0) / (np.float32(10000.0) ** (np.arange(0, 2 * half, 2, dtype=np.float32) / np.float32(2 * half)))).astype(np.float32)
        k[:, K_COL + col] = freq[p % half]
        k[:, K_COL + col + 1] = np.where(p % (2 * half) < half, -1.0, 1.0)
    k[:, K_COL + 4] = 1.0
    k[:, K_COL + 5] = np.pi / 2
    rel = np.arange(T)[None, :] - p[:, None]
    for h in range(RH):
        log_gamma = np.log1p(-(2.0 ** (-5.0 - h)))
        k[:, K_DECAY + h * T:K_DECAY + (h + 1) * T] = np.where(rel >= 0, np.exp(np.maximum(rel, 0) * log_gamma), 0.0) * P ** -0.5
    i, j = np.arange(P)[:, None] + P, np.arange(2 * P)[None, :]
    band = (i - j >= 0) & (i - j < P)
    for half in range(2):
        for b in range(2):
            seen = band & (j >= P) if half == b == 0 else band
            at = K_MASK + half * T + b * 2 * P
            k[:, at:at + 2 * P] = np.where(seen, 0.0, MASKED)
    return k


def decoder(nc, x, c, positions, norm_ffn1, norm_mix, norm_ffn2, final_norm, w_ada, b_ada,
            ffn1_w_up, ffn1_w_down, ffn2_w_up, ffn2_w_down, w_in, sinks, w_branch_ret,
            w_branch_swa, w_out, consts, out):
    F, R, I32 = mybir.dt.float32, mybir.dt.float32r, mybir.dt.int32
    ACT, ALU, AX = mybir.ActivationFunctionType, mybir.AluOpType, mybir.AxisListType
    ctx = ExitStack()
    with ctx:
        def sb(name, shape, dtype):
            return ctx.enter_context(nc.sbuf_tensor("sb_" + name, shape, dtype))

        def sem(name):
            return ctx.enter_context(nc.semaphore(name))

        XV = sb("x_or_values", [P, KT, T], F)
        Hhi, Hlo = sb("h_hi", [P, KT, T], R), sb("h_lo", [P, KT, T], R)
        Ahi, Alo = sb("a_hi", [P, 2 * KT, T], R), sb("a_lo", [P, 2 * KT, T], R)
        raw = [sb(f"raw{s}", [P, DOWN_UNIT], F) for s in range(2)]
        Whi = [sb(f"w_hi{s}", [P, DOWN_UNIT], R) for s in range(2)]
        Wlo = [sb(f"w_lo{s}", [P, DOWN_UNIT], R) for s in range(2)]
        K = sb("consts", [P, K_ALL], F)
        cos_r, sin_r = sb("cos_r", [P, T], F), sb("sin_r", [P, T], F)
        cos_s, sin_s = sb("cos_s", [P, T], F), sb("sin_s", [P, T], F)
        pos_i, pos_f = sb("pos_i", [P, T], I32), sb("pos_f", [P, T], F)
        vcols = sb("vector_cols", [P, 64 + 2 * MOD_TILES], F)
        c_act = sb("c_act", [P, KT], F)
        mod = sb("mod", [P, MOD_TILES], F)
        gain = sb("gain", [P, KT], F)
        half_gate = sb("half_gate", [P, KT], F)
        sink = sb("sinks", [P, DEPTH * QH], F)
        sm = sb("small", [P, 128], F)
        scratch = sb("scratch", [P, 12544], F)

        def view(at, n):
            return scratch[:, at:at + n]

        squares = view(0, 4096).rearrange("p (k t) -> p k t", t=T)
        merged_ret = squares
        ada_raw = [view(at, 1024).rearrange("p (k c) -> p k c", c=256) for at in (4096, 5120, 8448, 9472)]
        ada_acc = view(6144, 256)
        side, work = view(6400, 512), view(6912, 512)
        tbuf = [view(7424 + 512 * s, 512) for s in range(2)]
        xtok = view(0, 4096).rearrange("p (t d) -> p t d", d=D)
        vec_rows = view(6400, 384).rearrange("p (a c) -> p a c", c=P)
        out_tok = squares.rearrange("p k t -> p (k t)").rearrange("p (t d) -> p t d", d=D)
        k_all = view(0, 1280).rearrange("p (v t) -> p v t", v=2)
        k_cur = view(1280, 640)
        sv_all = view(1920, 512).rearrange("p (t v d) -> p v t d", v=2, d=HD)
        sv_cur = view(2432, 256).rearrange("p (t d) -> p t d", d=HD)
        v_cur = view(2688, 1024).rearrange("p (t e) -> p t e", e=DV)
        sq = view(3712, 1024).rearrange("p (s t) -> p s t", s=2)
        rq, rk = view(4736, 512), view(5248, 512)
        ret_s = [view(7424 + 512 * s, 512) for s in range(2)]
        probs = [view(8448 + 1024 * s, 1024) for s in range(2)]
        probs_t = view(10496, 1024)
        silu_g = view(11520, 1024).rearrange("p (e t) -> p e t", e=2)
        V = XV[:, :, :].rearrange("p (h e) t -> p h (e t)", h=RH).rearrange("p h (t e) -> p h t e", e=DV)

        ident, ones = K[:, K_ID:K_ID + P], K[:, K_COL + 4:K_COL + 5]
        rstd = sm[:, 0:16]
        rs_t, rs_v = sm[:, 16:32], sm[:, 32:48]
        smax, neg_m, sink_d, row_sum, exp_sink, rden = (
            [sm[:, 48 + 8 * n + 4 * s:52 + 8 * n + 4 * s] for s in range(2)] for n in range(6))
        neg_mean = sm[:, 96:112]

        pA = [ctx.enter_context(nc.psum_tensor(f"ps_proj{s}", [P, T], F)) for s in range(2)]
        pM = ctx.enter_context(nc.psum_tensor("ps_mid", [P, 4, T], F))
        pO = ctx.enter_context(nc.psum_tensor("ps_o", [P, T], F))
        pS = ctx.enter_context(nc.psum_tensor("ps_small", [P, T], F))
        pC = pM[:, 3, 0:2]

        x_spill = nc.dram_tensor("x_spill", [P, KT * T], F, kind="Internal").ap()

        const_in, x_in, tables_in = sem("const_in"), sem("x_in"), sem("tables_in")
        landed = [sem("landed0"), sem("landed1")]
        hi_ready, lo_ready = sem("hi_ready"), sem("lo_ready")
        unit_done = sem("unit_done")
        bank_free = [sem("bank_free0"), sem("bank_free1")]
        first_in, first_col, first_mod = [sem(f"first_in{s}") for s in range(4)], sem("first_col"), sem("first_mod")
        first_step = sem("first_step")
        ada_in, ada_used, ada_step = [sem("ada_in0"), sem("ada_in1")], sem("ada_used"), sem("ada_step")
        ada_sum, ada_col, mod_done = sem("ada_sum"), sem("ada_col"), sem("mod_done")
        cols_ps, cols_done, c_done = sem("cols_ps"), sem("cols_done"), sem("c_done")
        xt_ps, xt_done = sem("xt_ps"), sem("xt_done")
        ang_done, tables_done = sem("ang_done"), sem("tables_done")
        sq_ready, ss_ready, rstd_ready, rb_ready = sem("sq_ready"), sem("ss_ready"), sem("rstd_ready"), sem("rb_ready")
        t_ready, split_hi, split_lo = sem("t_ready"), sem("split_hi"), sem("split_lo")
        act_hi, act_lo = sem("act_hi"), sem("act_lo")
        x_out, x_back = sem("x_out"), sem("x_back")
        v_ps, v_mean, v_done = sem("v_ps"), sem("v_mean"), sem("v_done")
        sv_done, k_zero, k_done = sem("sv_done"), sem("k_zero"), sem("k_done")
        swapped, rope_done = sem("swapped"), sem("rope_done")
        key_in, head_in = sem("key_in"), sem("head_in")
        scores, max_ready, exp_ready, p_ready = sem("scores"), sem("max_ready"), sem("exp_ready"), sem("p_ready")
        pt_ps, pt_act, pt_dve, o_ps, o_hi, o_done = (sem(n) for n in ("pt_ps", "pt_act", "pt_dve", "o_ps", "o_hi", "o_done"))
        st_ps, st_done, y_ps, ysq, y_free, var_ps = (sem(n) for n in ("st_ps", "st_done", "y_ps", "ysq", "y_free", "var_ps"))
        mg_ready, mg_hi, mg_lo = sem("mg_ready"), sem("mg_hi"), sem("mg_lo")
        y_out, o_tok, stored = sem("y_out"), sem("o_tok"), sem("stored")
        carrier = {"pool": sem("pool_carrier"), "dve": sem("dve_carrier")}
        dve_step, act_step, pool_step = sem("dve_step"), sem("act_step"), sem("pool_step")

        up_v = [w.rearrange("l (k p) (g m c) -> l g m p k c", p=P, g=2, c=P) for w in (ffn1_w_up, ffn2_w_up)]
        down_v = [w.rearrange("l (h k p) (m c) -> l h m p k c", p=P, h=2, c=P) for w in (ffn1_w_down, ffn2_w_down)]
        in_v = w_in.rearrange("l (k p) (m c) -> l m p k c", p=P, c=P)
        rv_v = w_in.rearrange("l (j k p) n -> l j p k n", p=P, k=2)
        sq_v = {n: w.rearrange("l (k p) (m c) -> l m p k c", p=P, c=P)
                for n, w in (("ret", w_branch_ret), ("swa", w_branch_swa), ("out", w_out))}
        ada_v = w_ada.rearrange("l (s k p) (j c) -> l j s p k c", p=P, s=2, c=256)

        class Steps:

            def __init__(self, eng, own):
                self.eng, self.sem, self.base, self.n, self.made = eng, own, 0, 0, 0

            def mark(self, ins):
                ins.then_inc(self.sem, 1)
                self.n += 1
                self.made += 1

            def wait(self):
                self.eng.wait_ge(self.sem, self.base + self.n)

            @contextmanager
            def loop(self, first, end, each):
                start, made = self.base + self.n, self.made
                with self.eng.Fori(first, end) as i:
                    self.base, self.n = start + (i - first) * each, 0
                    yield i
                    assert self.made - made == each, self.made - made
                self.made = made + (end - first) * each
                self.base, self.n = start + (end - first) * each, 0

        def pair_no(l, off):
            return l * LAYER_PAIRS + off

        def gated_no(l, off):
            return l * LAYER_GATED + (off if off < HEAD0 else off - UNGATED)

        def job_no(l, q):
            return l * JOBS + q - FIRST_JOBS

        NORM_SPLIT = {"ffn1": 0, "mix": KT, "ret": 2 * KT, "ffn2": 3 * KT}
        NORM_NO = {"ffn1": 0, "mix": 1, "ret": 2, "ffn2": 3}
        NORM_SQ = {"ffn1": 0, "mix": KT, "ffn2": 2 * KT}
        MOD_COL = {"ffn1": 0, "mix": 3 * KT, "ffn2": 6 * KT}
        GAIN_COL = {"ffn1": 8, "mix": 24, "ffn2": 40, "final": 56}
        FFN = (("ffn1", 0), ("ffn2", FFN2))

        block = ctx.enter_context(nc.Block())

        @block.sync
        def _(sp):
            sp.dma_start(K[:, 0:K_DECAY], consts[:, 0:K_DECAY]).then_inc(const_in, 16)
            sp.dma_start(vec_rows[0:8, 0, :], c.rearrange("b (k p) -> (b k) p", p=P)).then_inc(const_in, 16)
            for n, w in enumerate((norm_ffn1, norm_mix, norm_ffn2)):
                sp.dma_start(vec_rows[8 + 16 * n:24 + 16 * n, 0, :], w.rearrange("l (k p) -> (l k) p", p=P)).then_inc(const_in, 16)
            sp.dma_start(vec_rows[56:64, 0, :], final_norm.rearrange("(k p) -> k p", p=P)).then_inc(const_in, 16)
            for l in range(DEPTH):
                sp.dma_start(vec_rows[0:MOD_TILES, 1 + l, :], b_ada[l].rearrange("(k p) -> k p", p=P)).then_inc(const_in, 16)
            sp.dma_start(pos_i[:, :], positions.broadcast_to([P, T])).then_inc(const_in, 16)
            sp.dma_start(xtok[:, :, :], x[0].rearrange("(t p) d -> p t d", p=P)).then_inc(x_in, 16)
            for r in range(FIRST_JOBS // 2):
                for n in range(4):
                    if r:
                        sp.wait_ge(first_step, 4 * (r - 1) + n + 1)
                    sp.dma_start(ada_raw[n], ada_v[0, 2 * r + n // 2, n % 2]).then_inc(first_in[n], 16)

            def load(b, s, src, k=KT):
                sp.wait_ge(lo_ready, 2 * b + s + 1)
                sp.dma_start(raw[s][:, 0:k * P].rearrange("p (k c) -> p k c", k=src.shape[1]), src).then_inc(landed[s], 16)

            def ffn_loads(l, f, half):
                name, first = FFN[f]
                b0 = pair_no(l, first + half * HALF_PAIRS)

                def up(i, b):
                    for s in range(2):
                        load(b, s, up_v[f][l, s, HALF * half + i])

                if f or half:
                    up(0, b0)
                with sp.Fori(1, HALF) as i:
                    up(i, b0 + i)
                with sp.Fori(0, KT // 2) as j:
                    for s in range(2):
                        load(b0 + HALF + j, s, down_v[f][l, half, 2 * j + s], HALF)

            def tables():
                sp.dma_start(K[:, K_DECAY:], consts[:, K_DECAY:]).then_inc(tables_in, 16)
                sp.dma_start(sink[:, :], sinks.rearrange("l h -> (l h)").unsqueeze(0).broadcast_to([P, DEPTH * QH])).then_inc(tables_in, 16)

            tables()
            with sp.Fori(0, DEPTH) as l:
                for s in range(2):
                    load(pair_no(l, 0), s, up_v[0][l, s, 0])
                ffn_loads(l, 0, 0)
                ffn_loads(l, 0, 1)
                for j in range(2 * V_PAIRS):
                    if j == 4:
                        sp.wait_ge(sq_ready, 3 * KT * l + 2 * KT)
                        sp.dma_start(x_spill, XV[:, :, :].rearrange("p k t -> p (k t)")).then_inc(x_out, 16)
                    at = RV_COL + T * (j // 4)
                    load(pair_no(l, MIX0 + j // 2), j % 2, rv_v[l, j % 4][:, :, at:at + T])
                load(pair_no(l, KV_PAIR), 0, in_v[l, SV])
                load(pair_no(l, KV_PAIR), 1, in_v[l, SK])
                with sp.Fori(0, RH) as i:
                    b = pair_no(l, HEAD0) + 3 * i
                    load(b, 0, in_v[l, SQ + 2 * i])
                    load(b, 1, in_v[l, SQ + 1 + 2 * i])
                    load(b + 1, 0, in_v[l, RQ + i])
                    load(b + 1, 1, in_v[l, RK + i])
                    load(b + 2, 0, in_v[l, RG + 2 * i])
                    load(b + 2, 1, in_v[l, RG + 1 + 2 * i])
                with sp.Fori(0, KT) as m:
                    load(pair_no(l, GATE_S0) + m, 0, in_v[l, GS + m])
                    load(pair_no(l, GATE_S0) + m, 1, sq_v["swa"][l, m])
                for first, end in ((0, 4), (4, KT)):
                    with sp.Fori(first, end) as m:
                        load(pair_no(l, GATE_R0) + m, 0, in_v[l, GR + m])
                        load(pair_no(l, GATE_R0) + m, 1, sq_v["ret"][l, m])
                    if first == 0:
                        sp.wait_ge(split_lo, LAYER_SPLITS * l + NORM_SPLIT["ffn2"])
                        sp.wait_ge(x_out, 16 * (l + 1))
                        sp.dma_start(XV[:, :, :].rearrange("p k t -> p (k t)"), x_spill).then_inc(x_back, 16)
                with sp.Fori(0, KT // 2) as j:
                    for s in range(2):
                        load(pair_no(l, OUT0) + j, s, sq_v["out"][l, 2 * j + s])
                ffn_loads(l, 1, 0)
                ffn_loads(l, 1, 1)
            for h in range(2):
                sp.wait_ge(o_tok, 4 * (h + 1))
                sp.dma_start(out[0].rearrange("(t p) d -> p t d", p=P)[:, :, 512 * h:512 * (h + 1)],
                             out_tok[:, :, 512 * h:512 * (h + 1)]).then_inc(stored, 16)
            sp.wait_ge(stored, 32)

        @block.gpsimd
        def _(pool):
            st = Steps(pool, pool_step)
            pool.wait_ge(const_in, 16 * 9)
            st.mark(pool.tensor_copy(pos_f[:, :], pos_i[:, :]))
            st.wait()
            for col, n, ang, tmp in ((0, cos_r, sin_r, cos_s), (2, cos_s, sin_s, pos_f)):
                def op(out, in0, *a):
                    st.mark(pool.tensor_scalar(out[:, :], in0[:, :], *a))
                    st.wait()

                op(ang, pos_f, K[:, K_COL + col:K_COL + col + 1], None, ALU.mult)
                op(n, ang, 1.0 / TWO_PI, ROUND, ALU.mult, ALU.add)
                op(n, n, ROUND, None, ALU.subtract)
                for part in (C1, C2, C3):
                    op(tmp, n, part, None, ALU.mult)
                    st.mark(pool.tensor_tensor(ang[:, :], ang[:, :], tmp[:, :], ALU.subtract))
                    st.wait()
                pool.tensor_scalar(ang[:, :], ang[:, :], float(np.float32(-3.1415925)), float(np.float32(3.1415925)),
                                   ALU.max, ALU.min).then_inc(ang_done, 1)
                pool.wait_ge(ang_done, 1 if col == 0 else 2)
            with pool.Fori(0, DEPTH) as l:
                pool.wait_ge(ss_ready, 3 * l + 2)
                pool.sem_inc(carrier["pool"], 1)
                pool.memset(k_all[:, :, 0:P], 0.0).then_inc(k_zero, 1)
                pool.wait_ge(k_zero, l + 1)
                pool.wait_ge(v_done, 2 * TT * (l + 1))
                pool.wait_ge(sv_done, l + 1)
                pool.wait_ge(k_done, l + 1)
                pool.sem_inc(carrier["pool"], 1)
                for kv in range(2):
                    with pool.Fori(0, 2) as r:
                        pool.wait_ge(unit_done, 2 * pair_no(l, HEAD0) + 12 * kv + 6 * r + 2)
                        pool.sem_inc(carrier["pool"], 1)
                        pool.tensor_copy(k_cur, k_all[:, kv, :]).then_inc(key_in, 1)
                        pool.wait_ge(y_ps, RH * l + 2 * kv + r + 1)
                        pool.sem_inc(carrier["pool"], 1)
                        pool.tensor_copy(sv_cur, sv_all[:, kv])
                        pool.tensor_copy(v_cur, V[:, 2 * kv + r]).then_inc(head_in, 1)

        @block.scalar
        def _(act):
            st = Steps(act, act_step)
            act.wait_ge(cols_done, 1)
            act.activation(c_act[:, :], vcols[:, 0:KT], ACT.Silu).then_inc(c_done, 1)
            for n, (cos, sin, col) in enumerate(((cos_r, sin_r, 1), (cos_s, sin_s, 3))):
                act.wait_ge(ang_done, 2)
                st.mark(act.activation(cos[:, :], sin[:, :], ACT.Abs))
                st.wait()
                act.activation(cos[:, :], cos[:, :], ACT.Sin, scale=-1.0, bias=K[:, K_COL + 5:K_COL + 6])
                act.activation(sin[:, :], sin[:, :], ACT.Sin, scale=K[:, K_COL + col:K_COL + col + 1]).then_inc(tables_done, 1)

            def split_weights(b, s, n):
                act.wait_ge(landed[s], 16 * (b + 1))
                act.wait_ge(unit_done, 2 * b + s + 1)
                act.activation(Whi[s][:, 0:n], raw[s][:, 0:n], ACT.Copy).then_inc(hi_ready, 1)

            def square(k, ready, value):
                act.wait_ge(ready, value)
                act.activation(squares[:, k, :], XV[:, k, :], ACT.Square).then_inc(sq_ready, 1)

            def load_job(l, q):
                for s in range(2):
                    act.wait_ge(ada_used, 2 * job_no(l, q) + s + 1)
                    act.dma_start(ada_raw[s], ada_v[l, q, s]).then_inc(ada_in[s], 16)

            def load_next_layers_job(l, n):
                with act.If(l < DEPTH - 1):
                    next_l = nc.s_assert_within(l + 1, 1, DEPTH - 1, skip_runtime_bounds_check_because="the last layer does not come here")
                    for s in range(2):
                        act.wait_ge(ada_used, 2 * job_no(l, JOBS + n) + s + 1)
                        act.dma_start(ada_raw[s], ada_v[next_l, n, s]).then_inc(ada_in[s], 16)

            def norm_hi(l, name):
                q = LAYER_SPLITS * l + NORM_SPLIT[name]
                for k in range(KT):
                    act.wait_ge(t_ready, q + k + 1)
                    shift = mod[:, MOD_COL[name] + k:MOD_COL[name] + k + 1]
                    act.activation(Hhi[:, k, :], tbuf[k % 2], ACT.Identity, bias=shift).then_inc(split_hi, 1)

            def ffn(l, f):
                name, first = FFN[f]
                for half in range(2):
                    b0, g0 = pair_no(l, first + half * HALF_PAIRS), gated_no(l, first + half * HALF_PAIRS)
                    a0 = FT * (2 * l + f) + HALF * half
                    q0 = FIRST_JOBS + HALF_JOBS * half

                    def up(i, n_next, load=None):
                        b, g = b0 + i, g0 + i
                        act.wait_ge(unit_done, 2 * b + 3)
                        act.wait_ge(bank_free[1], g + 1)
                        act.activation(side, pA[0][:, :], ACT.Silu).then_inc(bank_free[0], 1)
                        split_weights(b + 1, 0, n_next)
                        if load:
                            load(l, i)
                        split_weights(b + 1, 1, n_next)
                        act.wait_ge(bank_free[1], g + 2)
                        act.activation(Ahi[:, i, :], work, ACT.Copy).then_inc(act_hi, 1)

                    if f == 0:
                        with act.Fori(0, HALF - 1) as i:
                            up(i, UP_UNIT, lambda l, i: load_job(l, q0 + i))
                        up(HALF - 1, DOWN_UNIT, lambda l, i: load_job(l, q0 + i))
                    elif half == 0:
                        with act.Fori(0, FIRST_JOBS) as i:
                            up(i, UP_UNIT, load_next_layers_job)
                        with act.Fori(FIRST_JOBS, HALF - 1) as i:
                            up(i, UP_UNIT)
                        up(HALF - 1, DOWN_UNIT)
                    else:
                        with act.Fori(0, HALF - 1) as i:
                            up(i, UP_UNIT)
                        up(HALF - 1, DOWN_UNIT)

                    def down(j, n_next, load=None):
                        for s in range(2):
                            if n_next:
                                split_weights(b0 + HALF + j + 1, s, n_next)
                            if half == 1:
                                square(2 * j + s, bank_free[s], g0 + HALF + j + 2)
                            if load and s == 0:
                                load(l, j)

                    with act.Fori(0, KT // 2 - 1) as j:
                        down(j, DOWN_UNIT, (lambda l, j: load_job(l, q0 + HALF + j)) if f == 0 else None)
                    down(KT // 2 - 1, 0 if f == 1 and half == 1 else UP_UNIT)

            def swap(b, s, g, rope_no, ps, halves):
                act.wait_ge(unit_done, 2 * b + s + 3)
                act.wait_ge(rope_done, rope_no + 1)
                act.wait_ge(bank_free[1], g + 1)
                for at in range(0, P, 2 * halves):
                    act.activation(side[at:at + halves], ps[at + halves:at + 2 * halves, :], ACT.Copy)
                    last = act.activation(side[at + halves:at + 2 * halves], ps[at:at + halves, :], ACT.Copy)
                last.then_inc(swapped, 1)

            def exps(no, w):
                act.wait_ge(max_ready, no + 1)
                act.activation(exp_sink[w], sink_d[w], ACT.Exp)
                for n in range(4):
                    p = probs[w][:, 256 * n:256 * (n + 1)]
                    last = act.activation(p, p, ACT.Exp, bias=neg_m[w][:, n:n + 1], scale=HD ** -0.5,
                                          accum_out=row_sum[w][:, n:n + 1])
                last.then_inc(exp_ready, 1)

            def probs_out(no):
                act.wait_ge(pt_ps, 2 * no + 1)
                act.activation(probs_t[:, 0:T], pM[:, 2, :], ACT.Copy).then_inc(pt_act, 1)

            def swa_out(no, tile):
                act.wait_ge(o_ps, no + 1)
                act.activation(Ahi[:, KT + tile, :], pO[:, :], ACT.Copy).then_inc(o_hi, 1)

            def ret_hi(l, k):
                act.wait_ge(t_ready, LAYER_SPLITS * l + NORM_SPLIT["ret"] + k + 1)
                act.activation(Ahi[:, k, :], tbuf[0], ACT.Copy).then_inc(split_hi, 1)

            act.wait_ge(xt_ps, KT)
            for k in range(KT):
                square(k, xt_done, k + 1)
            act.wait_ge(first_mod, 1)
            with act.Fori(0, DEPTH) as l:
                for s in range(2):
                    split_weights(pair_no(l, 0), s, UP_UNIT)
                norm_hi(l, "ffn1")
                ffn(l, 0)
                norm_hi(l, "mix")
                for p in range(V_PAIRS):
                    if p % 2 == 1:
                        for s in range(2):
                            split_weights(pair_no(l, MIX0 + p + 1), s, UP_UNIT)
                        for tt in range(TT):
                            n = (p // 2) * TT + tt
                            act.wait_ge(v_mean, 2 * TT * l + n + 1)
                            act.wait_ge(x_out, 16 * (l + 1))
                            for h in range(2):
                                last = act.activation(V[:, 2 * (p // 2) + h, tt, :], pM[:, tt, DV * h:DV * (h + 1)],
                                                      ACT.Identity, bias=neg_mean[:, 2 * n + h:2 * n + h + 1])
                            last.then_inc(v_done, 1)
                    else:
                        for s in range(2):
                            split_weights(pair_no(l, MIX0 + p + 1), s, UP_UNIT)
                b, g = pair_no(l, KV_PAIR), gated_no(l, HEAD0)
                act.wait_ge(unit_done, 2 * b + 3)
                act.activation(sv_all.rearrange("p v t d -> p t v d"), pO[:, :].rearrange("p (t v d) -> p t v d", v=2, d=HD), ACT.Copy).then_inc(sv_done, 1)
                for s in range(2):
                    split_weights(b + 1, s, UP_UNIT)
                swap(b, 1, g, LAYER_ROPES * l, pS, HD // 2)
                def start_query(i, s):
                    b, g = pair_no(l, HEAD0) + 3 * i, gated_no(l, HEAD0) + 3 * i
                    swap(b, s, g, LAYER_ROPES * l + 1 + 4 * i + s, pA[s], HD // 2)
                    split_weights(b + 1, s, UP_UNIT)

                def middle(i):
                    b, g = pair_no(l, HEAD0) + 3 * i, gated_no(l, HEAD0) + 3 * i
                    rope0 = LAYER_ROPES * l + 1 + 4 * i
                    h0 = 4 * (RH * l + i)
                    exps(h0, 0)
                    swap(b + 1, 0, g + 1, rope0 + 2, pA[0], P // 2)
                    split_weights(b + 2, 0, UP_UNIT)
                    exps(h0 + 1, 1)
                    swap(b + 1, 1, g + 1, rope0 + 3, pA[1], P // 2)
                    split_weights(b + 2, 1, UP_UNIT)
                    probs_out(h0)
                    exps(h0 + 2, 0)
                    for s in range(2):
                        act.wait_ge(unit_done, 2 * (b + 2) + s + 3)
                        act.wait_ge(rope_done, rope0 + 4 + 1)
                        if s:
                            act.wait_ge(bank_free[0], g + 2 + 2)
                        act.activation(side, pA[s][:, :], ACT.Tanh, scale=0.5).then_inc(swapped, 1)
                        split_weights(b + 3, s, UP_UNIT)
                        if s == 0:
                            probs_out(h0 + 1)
                            exps(h0 + 3, 1)

                def tail(i, start):
                    h0 = 4 * (RH * l + i)
                    swa_out(2 * (RH * l + i), 2 * i)
                    probs_out(h0 + 2)
                    start(0)
                    probs_out(h0 + 3)
                    start(1)
                    swa_out(2 * (RH * l + i) + 1, 2 * i + 1)
                    act.wait_ge(y_ps, RH * l + i + 2)
                    for e in range(2):
                        act.activation(probs[1][:, T * e:T * (e + 1)], pM[:, 2 + e, :], ACT.Square).then_inc(ysq, 1)

                for s in range(2):
                    start_query(0, s)
                with act.Fori(0, RH - 1) as i:
                    middle(i)
                    tail(i, lambda s: start_query(i + 1, s))
                middle(RH - 1)
                tail(RH - 1, lambda s: None)
                with act.Fori(0, KT // 2) as j:
                    for s in range(2):
                        m = 2 * j + s
                        b, g = pair_no(l, GATE_S0) + m, gated_no(l, GATE_S0) + m
                        act.wait_ge(unit_done, 2 * b + 3)
                        act.wait_ge(bank_free[1], g + 1)
                        act.activation(side, pA[0][:, :], ACT.Tanh, scale=0.5).then_inc(bank_free[0], 1)
                        split_weights(b + 1, 0, UP_UNIT)
                        ret_hi(l, m)
                        split_weights(b + 1, 1, UP_UNIT)
                with act.Fori(0, KT) as m:
                    b, g = pair_no(l, GATE_R0) + m, gated_no(l, GATE_R0) + m
                    act.wait_ge(unit_done, 2 * b + 3)
                    act.wait_ge(bank_free[1], g + 1)
                    act.activation(side, pA[0][:, :], ACT.Tanh, scale=0.5).then_inc(bank_free[0], 1)
                    for s in range(2):
                        split_weights(b + 1, s, UP_UNIT)
                    act.wait_ge(mg_ready, KT * l + m + 1)
                    act.activation(Ahi[:, KT + m, :], work, ACT.Copy).then_inc(mg_hi, 1)
                with act.Fori(0, KT // 2) as j:
                    b, g = pair_no(l, OUT0) + j, gated_no(l, OUT0) + j
                    for s in range(2):
                        split_weights(b + 1, s, UP_UNIT)
                        square(2 * j + s, bank_free[s], g + 2)
                norm_hi(l, "ffn2")
                ffn(l, 1)
            for k in range(KT):
                act.wait_ge(y_out, k + 1)
                act.activation(out_tok[:, :, P * k:P * (k + 1)], pA[k % 2][:, :].rearrange("p (t c) -> p t c", c=P),
                               ACT.Copy).then_inc(o_tok, 1)

        @block.vector
        def _(dve):
            st = Steps(dve, dve_step)
            dve.sem_inc(lo_ready, 2)
            for s in range(2):
                dve.sem_inc(bank_free[s], 1)
            for own in (rope_done, mod_done, o_done, act_lo, mg_lo):
                dve.sem_inc(own, 1)
            dve.sem_inc(ada_used, 2)
            dve.sem_inc(y_free, 2)
            dve.wait_ge(cols_ps, 1)
            dve.tensor_copy(vcols[:, :], pS[:, 0:64 + 2 * MOD_TILES]).then_inc(cols_done, 1)
            for k in range(KT):
                dve.wait_ge(xt_ps, k + 1)
                dve.tensor_copy(XV[:, k, :], pA[k % 2][:, :]).then_inc(xt_done, 1)

            def split_weights(b, s, n):
                dve.wait_ge(hi_ready, 2 * b + s + 1)
                dve.tensor_tensor(Wlo[s][:, 0:n], raw[s][:, 0:n], Whi[s][:, 0:n].bitcast(F), ALU.subtract).then_inc(lo_ready, 1)

            def ada_sum_job(l, q):
                no = job_no(l, q)
                for k in range(KT):
                    s, col = k // 4, c_act[:, k:k + 1]
                    if k % 4 == 0:
                        dve.wait_ge(ada_in[s], 16 * (no + 1))
                    if k == 0:
                        ins = dve.tensor_scalar(ada_acc, ada_raw[0][:, 0, :], col, None, ALU.mult)
                    else:
                        ins = dve.scalar_tensor_tensor(ada_acc, ada_raw[s][:, k % 4, :], col, ada_acc, ALU.mult, ALU.add)
                    if k % 4 == 3:
                        ins.then_inc(ada_used, 1)
                        if s == 0:
                            dve.wait_ge(ada_used, 2 * no + 3)
                    else:
                        ins.then_inc(ada_step, 1)
                        dve.wait_ge(ada_step, 6 * no + k - s + 1)

            def ada_store_job(l, q, to, bias):
                dve.wait_ge(ada_col, job_no(l, q) + 1)
                dve.tensor_tensor(mod[:, bass.ds(2 * to, 2)], pC, vcols[:, bass.ds(64 + bias, 2)],
                                  ALU.add).then_inc(mod_done, 1)

            def rstd_of(n, scale, ready, value, last_scale=None):
                y, a, v = rstd[:, 0:n], rs_t[:, 0:n], rs_v[:, 0:n]
                dve.wait_ge(ready, value)
                chain = [
                    lambda: dve.tensor_scalar(v, pS[:, 0:n], scale, EPS, ALU.mult, ALU.add),
                    lambda: dve.tensor_scalar(y.bitcast(I32), v.bitcast(I32), 1, None, ALU.logical_shift_right),
                    lambda: dve.tensor_scalar(y.bitcast(I32), y.bitcast(I32), -1.0, float(0x5F3759DF), ALU.mult, ALU.add),
                ]
                for _ in range(3):
                    chain += [
                        lambda: dve.tensor_tensor(a, y, y, ALU.mult),
                        lambda: dve.scalar_tensor_tensor(a, a, -0.5, v, ALU.mult, ALU.mult),
                        lambda: dve.scalar_tensor_tensor(y, a, 1.5, y, ALU.add, ALU.mult),
                    ]
                if last_scale:
                    chain += [lambda: dve.tensor_scalar(y, y, last_scale, None, ALU.mult)]
                for op in chain[:-1]:
                    st.mark(op())
                    st.wait()
                chain[-1]().then_inc(rstd_ready, 1)

            def norm(l, name):
                at = MOD_COL[name]
                gcol = GAIN_COL[name]
                dve.wait_ge(mod_done, job_no(l, FIRST_JOBS if name == "ffn1" else JOBS) + 1)
                if name == "ffn1":
                    dve.wait_ge(first_mod, 1)
                st.mark(dve.scalar_tensor_tensor(gain[:, :], mod[:, at + KT:at + 2 * KT], 1.0,
                                                 vcols[:, bass.ds(gcol + KT * l, KT)], ALU.add, ALU.mult))
                no, q = 4 * l + NORM_NO[name], LAYER_SPLITS * l + NORM_SPLIT[name]
                rstd_of(TT, 1.0 / D, ss_ready, NORM_SQ[name] // KT + 3 * l + 1)
                dve.wait_ge(rb_ready, no + 1)

                def lo(k):
                    dve.wait_ge(split_hi, q + k + 1)
                    dve.scalar_tensor_tensor(Hlo[:, k, :], tbuf[k % 2], mod[:, at + k:at + k + 1],
                                             Hhi[:, k, :].bitcast(F), ALU.add, ALU.subtract).then_inc(split_lo, 1)

                for k in range(KT):
                    if k >= 2:
                        dve.wait_ge(split_lo, q + k - 1)
                    dve.scalar_tensor_tensor(tbuf[k % 2], pO[:, :], gain[:, k:k + 1], XV[:, k, :],
                                             ALU.mult, ALU.mult).then_inc(t_ready, 1)
                    if k:
                        lo(k - 1)
                lo(KT - 1)

            def add_gated(s, g, b, m):
                dve.wait_ge(unit_done, 2 * b + s + 3)
                dve.scalar_tensor_tensor(XV[:, m, :], pA[s][:, :], half_gate[:, bass.ds(m, 1)], XV[:, m, :],
                                         ALU.mult, ALU.add).then_inc(bank_free[s], 1)

            def halve_gate(l, name):
                at = MOD_COL[name] + 2 * KT
                dve.wait_ge(mod_done, job_no(l, FIRST_JOBS + HALF - 1 if name == "ffn1" else JOBS) + 1)
                st.mark(dve.tensor_scalar(half_gate[:, :], mod[:, at:at + KT], 0.5, None, ALU.mult))
                st.wait()
                dve.sem_inc(carrier["dve"], 1)

            def ffn(l, f):
                name, first = FFN[f]
                for half in range(2):
                    b0, g0 = pair_no(l, first + half * HALF_PAIRS), gated_no(l, first + half * HALF_PAIRS)
                    a0 = FT * (2 * l + f) + HALF * half
                    q0 = FIRST_JOBS + HALF_JOBS * half

                    def up(i, n_next, jobs=None):
                        b, g = b0 + i, g0 + i
                        split_weights(b + 1, 0, n_next)
                        dve.wait_ge(unit_done, 2 * b + 4)
                        dve.wait_ge(bank_free[0], g + 2)
                        dve.wait_ge(act_lo, a0 + i + 1)
                        dve.tensor_tensor(work, side, pA[1][:, :], ALU.mult).then_inc(bank_free[1], 1)
                        split_weights(b + 1, 1, n_next)
                        dve.wait_ge(act_hi, a0 + i + 1)
                        dve.tensor_tensor(Alo[:, i, :], work, Ahi[:, i, :].bitcast(F), ALU.subtract).then_inc(act_lo, 1)
                        if jobs:
                            jobs(i)

                    def store_job(n):
                        ada_store_job(l, q0 + n, q0 + n, MOD_TILES * l + 2 * (q0 + n))

                    def both_jobs(n):
                        store_job(n - 1)
                        ada_sum_job(l, q0 + n)

                    def next_layers_jobs(n, store=True, add=True):
                        with dve.If(l < DEPTH - 1):
                            if store:
                                ada_store_job(l, JOBS + n - 1, n - 1, nc.s_assert_within(
                                    MOD_TILES * (l + 1) + 2 * (n - 1), MOD_TILES, MOD_TILES * DEPTH - 2,
                                    skip_runtime_bounds_check_because="the last layer does not come here"))
                            if add:
                                ada_sum_job(l, JOBS + n)

                    if f == 0:
                        up(0, UP_UNIT, lambda n: ada_sum_job(l, q0))
                        with st.loop(1, HALF - 1, 0) as i:
                            up(i, UP_UNIT, both_jobs)
                        up(HALF - 1, DOWN_UNIT, both_jobs)
                    elif half == 0:
                        up(0, UP_UNIT, lambda n: next_layers_jobs(n, store=False))
                        with st.loop(1, FIRST_JOBS, 0) as i:
                            up(i, UP_UNIT, next_layers_jobs)
                        up(FIRST_JOBS, UP_UNIT, lambda n: next_layers_jobs(n, add=False))
                        with st.loop(FIRST_JOBS + 1, HALF - 1, 0) as i:
                            up(i, UP_UNIT)
                        up(HALF - 1, DOWN_UNIT)
                    else:
                        with st.loop(0, HALF - 1, 0) as i:
                            up(i, UP_UNIT)
                        up(HALF - 1, DOWN_UNIT)
                    if half == 0:
                        halve_gate(l, name)

                    def down(j, n_next):
                        for s in range(2):
                            add_gated(s, g0 + HALF + j, b0 + HALF + j, 2 * j + s)
                            if n_next:
                                split_weights(b0 + HALF + j + 1, s, n_next)

                    with st.loop(0, KT // 2 - 1, 0) as j:
                        down(j, DOWN_UNIT)
                        if f == 0:
                            both_jobs(HALF + j)
                    down(KT // 2 - 1, 0 if f == 1 and half == 1 else UP_UNIT)
                    if f == 0:
                        store_job(HALF_JOBS - 1)

            def rope(no, side_no, ps, cos, sin, outs, s=None):
                dve.wait_ge(swapped, side_no + 1)
                dve.wait_ge(rope_done, no + 1)
                first = dve.tensor_tensor(work, ps[:, :], cos[:, :], ALU.mult)
                if s is None:
                    st.mark(first)
                else:
                    first.then_inc(bank_free[s], 1)
                st.mark(dve.tensor_tensor(side, side, sin[:, :], ALU.mult))
                st.wait()
                for to, p0, p1 in outs:
                    last = dve.tensor_tensor(to, work[p0:p1], side[p0:p1], ALU.add)
                last.then_inc(rope_done, 1)

            def maxima(no, l, i, t, half, w):
                dve.wait_ge(scores, no + 1)
                mask = K[:, K_MASK + T * half:K_MASK + T * (half + 1)]
                st.mark(dve.tensor_tensor(probs[w].rearrange("p (a t) -> p a t", a=2), pM[:, 0:2, :],
                                          mask.unsqueeze(1).broadcast_to([P, 2, T]), ALU.add))
                st.wait()
                st.mark(dve.reduce_max(smax[w], probs[w].rearrange("p (n k) -> p n k", n=4), AX.X))
                st.wait()
                neg_sink = sink[:, bass.ds(QH * l + 4 * i + 2 * t, 2)].unsqueeze(2).broadcast_to([P, 2, 2])

                def two(a):
                    return a.rearrange("p (a b) -> p a b", a=2)

                st.mark(dve.scalar_tensor_tensor(two(neg_m[w]), two(smax[w]), -(HD ** -0.5), neg_sink, ALU.mult, ALU.min))
                st.wait()
                dve.tensor_tensor(two(sink_d[w]), two(neg_m[w]), neg_sink, ALU.subtract).then_inc(max_ready, 1)

            def normalise(no, w):
                dve.wait_ge(exp_ready, no + 1)
                st.mark(dve.tensor_tensor(rden[w], row_sum[w], exp_sink[w], ALU.add))
                st.wait()
                st.mark(dve.reciprocal(rden[w], rden[w]))
                st.wait()
                for n in range(4):
                    p = probs[w][:, 256 * n:256 * (n + 1)]
                    last = dve.tensor_scalar(p, p, rden[w][:, n:n + 1], None, ALU.mult)
                last.then_inc(p_ready, 1)

            def probs_out(no):
                dve.wait_ge(pt_ps, 2 * no + 2)
                dve.tensor_copy(probs_t[:, T:2 * T], pM[:, 3, :]).then_inc(pt_dve, 1)

            def swa_out(no, tile):
                dve.wait_ge(o_hi, no + 1)
                dve.tensor_tensor(Alo[:, KT + tile, :], pO[:, :], Ahi[:, KT + tile, :].bitcast(F), ALU.subtract).then_inc(o_done, 1)

            dve.wait_ge(first_col, 1)
            dve.tensor_tensor(mod[:, 0:2 * FIRST_JOBS], pM[:, 3, 0:2 * FIRST_JOBS], vcols[:, 64:64 + 2 * FIRST_JOBS],
                              ALU.add).then_inc(first_mod, 1)
            dve.wait_ge(tables_in, 32)
            st.mark(dve.tensor_scalar(sink[:, :], sink[:, :], -1.0, None, ALU.mult))
            st.wait()
            with st.loop(0, DEPTH, LAYER_STEPS) as l:
                for s in range(2):
                    split_weights(pair_no(l, 0), s, UP_UNIT)
                norm(l, "ffn1")
                ffn(l, 0)
                norm(l, "mix")
                for p in range(V_PAIRS):
                    for s in range(2):
                        split_weights(pair_no(l, MIX0 + p + 1), s, UP_UNIT)
                    if p % 2 == 1:
                        for tt in range(TT):
                            n = (p // 2) * TT + tt
                            m = neg_mean[:, 2 * n:2 * n + 2]
                            if tt < TT - 1:
                                dve.wait_ge(v_ps, 2 * (TT - 1) * l + (TT - 1) * (p // 2) + tt + 1)
                            else:
                                dve.wait_ge(unit_done, 2 * pair_no(l, MIX0 + p) + 4)
                            st.mark(dve.reduce_sum(m, pM[:, tt, :].rearrange("p (h e) -> p h e", h=2), AX.X))
                            st.wait()
                            dve.tensor_scalar(m, m, -1.0 / DV, None, ALU.mult).then_inc(v_mean, 1)
                b = pair_no(l, KV_PAIR)
                for s in range(2):
                    split_weights(b + 1, s, UP_UNIT)
                dve.wait_ge(tables_done, 2)
                dve.wait_ge(k_zero, l + 1)
                rope(LAYER_ROPES * l, 25 * l, pS, cos_s, sin_s,
                     [(k_all[64 * h:64 * (h + 1), v, P:], 64 * v, 64 * (v + 1)) for v in range(2) for h in range(2)])
                dve.wait_ge(rope_done, LAYER_ROPES * l + 2)
                dve.sem_inc(k_done, 1)
                def numbers(i):
                    return (pair_no(l, HEAD0) + 3 * i, 25 * l + 1 + 6 * i, LAYER_ROPES * l + 1 + 4 * i, RH * l + i)

                def start_query(i, s):
                    b, side0, rope0, n0 = numbers(i)
                    rope(rope0 + s, side0 + s, pA[s], cos_s, sin_s, [(sq[:, s, :], 0, P)], s)

                def middle(i):
                    b, side0, rope0, n0 = numbers(i)
                    h0 = 4 * n0

                    def retention_rope(n, tile):
                        rope(rope0 + 2 + n, side0 + 2 + n, pA[n], cos_r, sin_r, [(tile, 0, P)], n)
                        split_weights(b + 2, n, UP_UNIT)

                    def retention_gate(n):
                        dve.wait_ge(swapped, side0 + 4 + n + 1)
                        dve.scalar_tensor_tensor(silu_g[:, n, :], side, 1.0, pA[n][:, :], ALU.add, ALU.mult).then_inc(bank_free[n], 1)
                        split_weights(b + 3, n, UP_UNIT)

                    maxima(h0, l, i, 0, 0, 0)
                    retention_rope(0, rq)
                    normalise(h0, 0)
                    maxima(h0 + 1, l, i, 0, 1, 1)
                    retention_rope(1, rk)
                    probs_out(h0)
                    maxima(h0 + 2, l, i, 1, 0, 0)
                    normalise(h0 + 1, 1)
                    retention_gate(0)
                    probs_out(h0 + 1)
                    maxima(h0 + 3, l, i, 1, 1, 1)
                    normalise(h0 + 2, 0)
                    retention_gate(1)
                    normalise(h0 + 3, 1)

                def tail(i, next_head):
                    b, side0, rope0, n0 = numbers(i)
                    h0 = 4 * n0

                    def decay(n):
                        w = T - P * n
                        dve.wait_ge(st_ps, TT * n0 + n + 1)
                        dve.tensor_tensor(ret_s[n % 2][:, 0:w], pM[:, n % 2, 0:w], K[:, bass.ds(K_DECAY + T * i, w)],
                                          ALU.mult).then_inc(st_done, 1)

                    swa_out(2 * n0, 2 * i)
                    probs_out(h0 + 2)
                    decay(0)
                    decay(1)
                    if next_head:
                        start_query(i + 1, 0)
                        split_weights(b + 4, 0, UP_UNIT)
                    probs_out(h0 + 3)
                    if next_head:
                        start_query(i + 1, 1)
                    swa_out(2 * n0 + 1, 2 * i + 1)
                    decay(2)
                    decay(3)
                    if next_head:
                        split_weights(b + 4, 1, UP_UNIT)
                    for e in range(2):
                        dve.wait_ge(ysq, 2 * n0 + e + 1)
                        dve.tensor_tensor(XV[:, 2 * i + e, :], pM[:, 2 + e, :], silu_g[:, e, :], ALU.mult).then_inc(y_free, 1)

                for s in range(2):
                    start_query(0, s)
                    split_weights(b + 2, s, UP_UNIT)
                with st.loop(0, RH - 1, 4 + 4 * 5) as i:
                    middle(i)
                    tail(i, True)
                middle(RH - 1)
                tail(RH - 1, False)
                rstd_of(TT * RH, 1.0 / DV, var_ps, RH * (l + 1), 0.5)
                with st.loop(0, KT // 2, 0) as j:
                    for s in range(2):
                        m = 2 * j + s
                        b, g = pair_no(l, GATE_S0) + m, gated_no(l, GATE_S0) + m
                        q = LAYER_SPLITS * l + NORM_SPLIT["ret"] + m
                        split_weights(b + 1, 0, UP_UNIT)
                        dve.wait_ge(bank_free[0], g + 2)
                        dve.wait_ge(unit_done, 2 * b + 4)
                        dve.scalar_tensor_tensor(merged_ret[:, m, :], side, 1.0, pA[1][:, :], ALU.add, ALU.mult).then_inc(bank_free[1], 1)
                        dve.wait_ge(rb_ready, 4 * l + 3)
                        dve.wait_ge(split_lo, q)
                        dve.tensor_tensor(tbuf[0], XV[:, m, :], pM[:, bass.ds(j, 1), :].rearrange("p a t -> p (a t)"), ALU.mult).then_inc(t_ready, 1)
                        split_weights(b + 1, 1, UP_UNIT)
                        dve.wait_ge(split_hi, q + 1)
                        dve.tensor_tensor(Alo[:, m, :], tbuf[0], Ahi[:, m, :].bitcast(F), ALU.subtract).then_inc(split_lo, 1)
                with st.loop(0, KT, 0) as m:
                    b, g = pair_no(l, GATE_R0) + m, gated_no(l, GATE_R0) + m
                    split_weights(b + 1, 0, UP_UNIT)
                    dve.wait_ge(bank_free[0], g + 2)
                    dve.wait_ge(unit_done, 2 * b + 4)
                    dve.wait_ge(mg_lo, KT * l + m + 1)
                    dve.scalar_tensor_tensor(work, side, 1.0, pA[1][:, :], ALU.add, ALU.mult).then_inc(bank_free[1], 1)
                    dve.wait_ge(bank_free[1], g + 2)
                    dve.tensor_tensor(work, work, merged_ret[:, m, :], ALU.add).then_inc(mg_ready, 1)
                    split_weights(b + 1, 1, UP_UNIT)
                    dve.wait_ge(mg_hi, KT * l + m + 1)
                    dve.tensor_tensor(Alo[:, KT + m, :], work, Ahi[:, KT + m, :].bitcast(F), ALU.subtract).then_inc(mg_lo, 1)
                dve.wait_ge(x_back, 16 * (l + 1))
                halve_gate(l, "mix")
                with st.loop(0, KT // 2, 0) as j:
                    b, g = pair_no(l, OUT0) + j, gated_no(l, OUT0) + j
                    for s in range(2):
                        add_gated(s, g, b, 2 * j + s)
                        split_weights(b + 1, s, UP_UNIT)
                norm(l, "ffn2")
                ffn(l, 1)
            rstd_of(TT, 1.0 / D, ss_ready, 3 * DEPTH + 1)
            dve.wait_ge(rb_ready, 4 * DEPTH + 1)
            for k in range(KT):
                if k >= 2:
                    dve.wait_ge(y_out, k - 1)
                g = vcols[:, GAIN_COL["final"] + k:GAIN_COL["final"] + k + 1]
                dve.scalar_tensor_tensor(tbuf[k % 2], pO[:, :], g, XV[:, k, :], ALU.mult, ALU.mult).then_inc(t_ready, 1)

        @block.tensor
        def _(pe):
            pe.sem_inc(unit_done, 2)
            pe.sem_inc(y_ps, 1)
            pe.wait_ge(const_in, 16 * 9)
            pe.transpose(pS[:, 0:64], vec_rows[0:64, 0, :], ident[0:64, 0:64])
            for n in range(DEPTH):
                last = pe.transpose(pS[:, 64 + MOD_TILES * n:64 + MOD_TILES * (n + 1)], vec_rows[0:MOD_TILES, 1 + n, :],
                                    ident[0:MOD_TILES, 0:MOD_TILES])
            last.then_inc(cols_ps, 1)
            pe.wait_ge(x_in, 16)
            for k in range(KT):
                if k >= 2:
                    pe.wait_ge(xt_done, k - 1)
                for t in range(TT):
                    last = pe.transpose(pA[k % 2][:, P * t:P * (t + 1)], xtok[:, t, P * k:P * (k + 1)], ident)
                last.then_inc(xt_ps, 1)

            pe.wait_ge(c_done, 1)
            for r in range(FIRST_JOBS // 2):
                for n in range(4):
                    pe.wait_ge(first_in[n], 16 * (r + 1))
                    for kk in range(4):
                        k = 4 * (n % 2) + kk
                        for half in range(2):
                            col = 2 * (2 * r + n // 2) + half
                            last = pe.matmul(pM[:, 3, col:col + 1], ada_raw[n][:, kk, P * half:P * (half + 1)], c_act[:, k:k + 1],
                                             start=(r == n == kk == half == 0), stop=(k == KT - 1), skip_group_check=True)
                    last.then_inc(*((first_step, 1) if r < FIRST_JOBS // 2 - 1 or n < 3 else (first_col, 1)))

            def product(bank, s, k, hi, lo, first, last):
                w = slice(P * k, P * (k + 1))
                pe.matmul(bank, Whi[s][:, w], hi, start=first, stop=False)
                pe.matmul(bank, Whi[s][:, w], lo, start=False, stop=False)
                return pe.matmul(bank, Wlo[s][:, w], hi, start=False, stop=last)

            def h_tile(k):
                return Hhi[:, k, :], Hlo[:, k, :]

            def a_tile(k):
                return Ahi[:, k, :], Alo[:, k, :]

            def start_unit(b, g, s):
                pe.wait_ge(lo_ready, 2 * b + s + 3)
                pe.wait_ge(bank_free[s], g + 1)

            def unit(b, g, s, tiles, at=0, n=KT, waits={}):
                start_unit(b, g, s)
                for k in range(n):
                    if k in waits:
                        pe.wait_ge(*waits[k])
                    last = product(pA[s][:, :], s, k, *tiles(at + k), k == 0, k == n - 1)
                last.then_inc(unit_done, 1)

            def ada_job(l, q):
                pe.wait_ge(ada_used, 2 * job_no(l, q) + 4)
                pe.wait_ge(mod_done, job_no(l, q) + 1)
                for n in range(2):
                    last = pe.matmul(pC[:, n:n + 1], ada_acc[:, P * n:P * (n + 1)], ones, start=True, stop=True)
                last.then_inc(ada_col, 1)

            def spread_rstd(no, bank, at):
                pe.wait_ge(rstd_ready, no + 1)
                for t in range(TT):
                    last = pe.matmul(bank[:, P * t:P * (t + 1)], rstd[:, at + t:at + t + 1].broadcast_to([P, P]), ident,
                                     start=True, stop=True)
                return last

            def norm(no, sq0):
                for k in range(KT):
                    pe.wait_ge(sq_ready, sq0 + k + 1)
                    for t in range(TT):
                        last = pe.matmul(pS[:, t:t + 1], squares[:, k, P * t:P * (t + 1)], ones,
                                         start=(k == 0 and t == 0), stop=(k == KT - 1), skip_group_check=True)
                last.then_inc(ss_ready, 1)
                spread_rstd(no, pO, 0).then_inc(rb_ready, 1)

            def ffn(l, f):
                name, first = FFN[f]
                for half in range(2):
                    b0, g0 = pair_no(l, first + half * HALF_PAIRS), gated_no(l, first + half * HALF_PAIRS)
                    a0 = FT * (2 * l + f) + HALF * half
                    q0 = FIRST_JOBS + HALF_JOBS * half
                    for s in range(2):
                        start_unit(b0, g0, s)
                    for k in range(KT):
                        if half == 0:
                            pe.wait_ge(split_lo, LAYER_SPLITS * l + NORM_SPLIT[name] + k + 1)
                        for s in range(2):
                            last = product(pA[s][:, :], s, k, *h_tile(k), k == 0, k == KT - 1)
                            if k == KT - 1:
                                last.then_inc(unit_done, 1)
                    with pe.Fori(1, FIRST_JOBS + 1 if f and half == 0 else HALF) as i:
                        for s in range(2):
                            unit(b0 + i, g0 + i, s, h_tile)
                        if f == 0:
                            ada_job(l, q0 + i - 1)
                        elif half == 0:
                            with pe.If(l < DEPTH - 1):
                                ada_job(l, JOBS + i - 1)
                    if f and half == 0:
                        with pe.Fori(FIRST_JOBS + 1, HALF) as i:
                            for s in range(2):
                                unit(b0 + i, g0 + i, s, h_tile)
                    with pe.Fori(0, KT // 2) as j:
                        for s in range(2):
                            unit(b0 + HALF + j, g0 + HALF + j, s, a_tile, 0, HALF,
                                 {0: (act_lo, a0 + HALF), HALF - 1: (act_lo, a0 + HALF + 1)})
                        if f == 0:
                            ada_job(l, q0 + HALF - 1 + j)

            def swa_scores(no, t, half):
                for n in range(2):
                    blk = 2 * half + n
                    for a in range(2):
                        p = slice(HD * a, HD * (a + 1))
                        last = pe.matmul(pM[:, a, 256 * n:256 * (n + 1)], sq[p, t, P * blk:P * (blk + 1)],
                                         k_cur[p, P * blk:P * (blk + 2)], start=True, stop=True)
                last.then_inc(scores, 1)

            def swa_transposes(no, w):
                pe.wait_ge(p_ready, no + 1)
                for a in range(2):
                    for n in range(4):
                        last = pe.transpose(pM[:, 2 + a, P * n:P * (n + 1)], probs[w][:, T * a + P * n:T * a + P * (n + 1)], ident)
                    last.then_inc(pt_ps, 1)

            def swa_values(no, half):
                pe.wait_ge(pt_act, no + 1)
                pe.wait_ge(pt_dve, no + 1)
                for n in range(2):
                    blk = 2 * half + n
                    for kt in range(0 if blk else 1, 2):
                        for a in range(2):
                            at = T * a + 256 * n + P * kt
                            last = pe.matmul(pO[HD * a:HD * (a + 1), P * blk:P * (blk + 1)], sv_cur[:, blk - 1 + kt, :],
                                             probs_t[:, at:at + P], start=(kt == (0 if blk else 1)), stop=(kt == 1))
                return last

            with pe.Fori(0, DEPTH) as l:
                norm(4 * l, 3 * KT * l)
                ffn(l, 0)
                norm(4 * l + 1, 3 * KT * l + KT)
                for j in range(2 * V_PAIRS):
                    b, s = pair_no(l, MIX0 + j // 2), j % 2
                    pe.wait_ge(lo_ready, 2 * b + s + 3)
                    for t in range(TT):
                        if j == 4:
                            pe.wait_ge(v_done, 2 * TT * l + t + 1)
                        for kk in range(2):
                            k = 2 * (j % 4) + kk
                            if j < 4 and t == 0:
                                pe.wait_ge(split_lo, LAYER_SPLITS * l + NORM_SPLIT["mix"] + k + 1)
                            w, tok = slice(T * kk, T * (kk + 1)), slice(P * t, P * (t + 1))
                            pe.matmul(pM[:, t, :], Hhi[:, k, tok], Whi[s][:, w], start=(k == 0), stop=False)
                            pe.matmul(pM[:, t, :], Hhi[:, k, tok], Wlo[s][:, w], start=False, stop=False)
                            last = pe.matmul(pM[:, t, :], Hlo[:, k, tok], Whi[s][:, w], start=False, stop=(k == KT - 1))
                        if j % 4 == 3 and t < TT - 1:
                            last.then_inc(v_ps, 1)
                    last.then_inc(unit_done, 1)
                b = pair_no(l, KV_PAIR)
                pe.wait_ge(lo_ready, 2 * b + 3)
                for t in range(TT):
                    for k in range(KT):
                        w, tok = slice(P * k, P * (k + 1)), slice(P * t, P * (t + 1))
                        o = pO[:, P * t:P * (t + 1)]
                        pe.matmul(o, Hhi[:, k, tok], Whi[0][:, w], start=(k == 0), stop=False)
                        pe.matmul(o, Hhi[:, k, tok], Wlo[0][:, w], start=False, stop=False)
                        last = pe.matmul(o, Hlo[:, k, tok], Whi[0][:, w], start=False, stop=(k == KT - 1))
                last.then_inc(unit_done, 1)
                pe.wait_ge(lo_ready, 2 * b + 4)
                for k in range(KT):
                    last = product(pS[:, :], 1, k, *h_tile(k), k == 0, k == KT - 1)
                last.then_inc(unit_done, 1)
                def numbers(i):
                    return (pair_no(l, HEAD0) + 3 * i, gated_no(l, HEAD0) + 3 * i, LAYER_ROPES * l + 1 + 4 * i, RH * l + i)

                def start_attention(i):
                    b, g, rope0, n0 = numbers(i)
                    pe.wait_ge(key_in, n0 + 1)
                    pe.wait_ge(rope_done, rope0 + 2)
                    swa_scores(4 * n0, 0, 0)
                    unit(b + 1, g + 1, 0, h_tile)

                def middle(i):
                    b, g, rope0, n0 = numbers(i)
                    h0, o0 = 4 * n0, 2 * n0
                    pe.wait_ge(max_ready, h0 + 1)
                    swa_scores(h0 + 1, 0, 1)
                    unit(b + 1, g + 1, 1, h_tile)
                    pe.wait_ge(y_free, 2 * n0 + 2)
                    swa_transposes(h0, 0)
                    pe.wait_ge(rope_done, rope0 + 3)
                    pe.wait_ge(max_ready, h0 + 2)
                    swa_scores(h0 + 2, 1, 0)
                    unit(b + 2, g + 2, 0, h_tile)
                    pe.wait_ge(o_done, o0 + 1)
                    pe.wait_ge(head_in, n0 + 1)
                    swa_values(h0, 0)
                    swa_transposes(h0 + 1, 1)
                    pe.wait_ge(max_ready, h0 + 3)
                    swa_scores(h0 + 3, 1, 1)
                    unit(b + 2, g + 2, 1, h_tile)

                def tail(i, unit_0, unit_1):
                    b, g, rope0, n0 = numbers(i)
                    h0, o0 = 4 * n0, 2 * n0

                    def ret_scores(n):
                        pe.matmul(pM[:, n % 2, 0:T - P * n], rk[:, P * n:P * (n + 1)], rq[:, P * n:T],
                                  start=True, stop=True).then_inc(st_ps, 1)

                    def ret_values(n):
                        pe.wait_ge(st_done, TT * n0 + n + 1)
                        for e in range(2):
                            last = pe.matmul(pM[:, 2 + e, P * n:T], v_cur[:, n, P * e:P * (e + 1)], ret_s[n % 2][:, 0:T - P * n],
                                             start=(n == 0), stop=(n == TT - 1))
                        return last

                    swa_values(h0 + 1, 1).then_inc(o_ps, 1)
                    swa_transposes(h0 + 2, 0)
                    pe.wait_ge(max_ready, h0 + 4)
                    pe.wait_ge(rope_done, rope0 + 5)
                    ret_scores(0)
                    ret_scores(1)
                    unit_0()
                    pe.wait_ge(o_done, o0 + 2)
                    swa_values(h0 + 2, 0)
                    swa_transposes(h0 + 3, 1)
                    unit_1()
                    swa_values(h0 + 3, 1).then_inc(o_ps, 1)
                    ret_values(0)
                    ret_scores(2)
                    ret_values(1)
                    ret_scores(3)
                    ret_values(2)
                    ret_values(3).then_inc(y_ps, 1)

                def variance(i):
                    n0 = RH * l + i
                    pe.wait_ge(ysq, 2 * n0 + 2)
                    for t in range(TT):
                        for e in range(2):
                            last = pe.matmul(pS[:, bass.ds(TT * i + t, 1)], probs[1][:, T * e + P * t:T * e + P * (t + 1)], ones,
                                             start=(e == 0), stop=(e == 1))
                    last.then_inc(var_ps, 1)

                for s in range(2):
                    unit(b + 1, gated_no(l, HEAD0), s, h_tile)
                start_attention(0)
                with pe.Fori(0, RH - 1) as i:
                    b, g, rope0, n0 = numbers(i + 1)
                    middle(i)
                    tail(i, lambda: unit(b, g, 0, h_tile), lambda: unit(b, g, 1, h_tile))
                    start_attention(i + 1)
                    variance(i)
                middle(RH - 1)
                b, g = pair_no(l, GATE_S0), gated_no(l, GATE_S0)
                tail(RH - 1, lambda: unit(b, g, 0, h_tile), lambda: None)
                variance(RH - 1)
                unit(b, g, 1, a_tile, KT, KT, {0: (o_done, 2 * RH * (l + 1) + 1)})
                pe.wait_ge(y_free, 2 * RH * (l + 1) + 2)
                for h in range(RH):
                    last = spread_rstd(4 * l + 2, pM[:, h, :], TT * h)
                last.then_inc(rb_ready, 1)
                with pe.Fori(1, KT) as m:
                    unit(b + m, g + m, 0, h_tile)
                    unit(b + m, g + m, 1, a_tile, KT)
                b, g = pair_no(l, GATE_R0), gated_no(l, GATE_R0)
                with pe.Fori(0, KT) as m:
                    unit(b + m, g + m, 0, h_tile)
                    unit(b + m, g + m, 1, a_tile, 0, KT, {0: (split_lo, LAYER_SPLITS * l + NORM_SPLIT["ffn2"])})
                b, g = pair_no(l, OUT0), gated_no(l, OUT0)
                with pe.Fori(0, KT // 2) as j:
                    for s in range(2):
                        unit(b + j, g + j, s, a_tile, KT, KT, {0: (mg_lo, KT * (l + 1)), KT - 1: (mg_lo, KT * (l + 1) + 1)})
                norm(4 * l + 3, 3 * KT * l + 2 * KT)
                ffn(l, 1)
            norm(4 * DEPTH, 3 * KT * DEPTH)
            for k in range(KT):
                pe.wait_ge(t_ready, LAYER_SPLITS * DEPTH + k + 1)
                if k >= 2:
                    pe.wait_ge(o_tok, k - 1)
                for t in range(TT):
                    last = pe.transpose(pA[k % 2][:, P * t:P * (t + 1)], tbuf[k % 2][:, P * t:P * (t + 1)], ident)
                last.then_inc(y_out, 1)


_INS = ['x', 'c', 'positions', 'norm_ffn1', 'norm_mix', 'norm_ffn2', 'final_norm', 'w_ada', 'b_ada',
        'ffn1_w_up', 'ffn1_w_down', 'ffn2_w_up', 'ffn2_w_down', 'w_in', 'sinks', 'w_branch_ret',
        'w_branch_swa', 'w_out']


def kernel(**inputs):
    import concourse.bacc as bacc
    from concourse.bass_utils import run_bass_kernel_spmd

    nc = bacc.Bacc("TRN2", target_bir_lowering=False, num_devices=1, dynamic_dma_scratch_size=1024)
    arrays = {f"in_{n}": np.ascontiguousarray(inputs[n]) for n in _INS}
    arrays["in_consts"] = constants()
    args = [nc.dram_tensor(n, a.shape, mybir.dt.from_np(a.dtype), kind="ExternalInput").ap() for n, a in arrays.items()]
    args.append(nc.dram_tensor("out_0", (1, T, D), mybir.dt.float32, kind="ExternalOutput").ap())
    decoder(nc, *args)
    r = run_bass_kernel_spmd(nc, [arrays], core_ids=[0])
    return r.results[0]["out_0"]
```

```python
import numpy as np

import concourse.bass as bass
from concourse import mybir
from contextlib import ExitStack, contextmanager

D, T, DEPTH, P = 1024, 512, 2, 128
FF = 2816
KT = D // P
TT = T // P
FT = FF // P
HALF = FT // 2
RH, DV = 4, 256
QH, HD = 16, 64
EPS = 1e-6
MOD_TILES = 9 * KT
RQ, RK, RG, SQ, SK, SV, GR, GS = 0, 4, 16, 24, 32, 33, 34, 42
RV_COL = 1024
UP_UNIT, DOWN_UNIT = KT * P, HALF * P

HALF_PAIRS = HALF + KT // 2
FFN_PAIRS = 2 * HALF_PAIRS
V_PAIRS = 4
MIX0 = FFN_PAIRS
KV_PAIR = MIX0 + V_PAIRS
HEAD0 = KV_PAIR + 1
GATE_S0 = HEAD0 + 3 * RH
GATE_R0 = GATE_S0 + KT
OUT0 = GATE_R0 + KT
FFN2 = OUT0 + KT // 2
LAYER_PAIRS = FFN2 + FFN_PAIRS
UNGATED = V_PAIRS + 1
LAYER_GATED = LAYER_PAIRS - UNGATED
JOBS, FIRST_JOBS = 36, 8
PE_JOBS, DVE_JOBS = (0, 3, 6), (1, 2, 4, 5, 7)
HALF_JOBS = (JOBS - FIRST_JOBS) // 2
LAYER_SPLITS = 4 * KT
LAYER_ROPES = 1 + 4 * RH
LAYER_SIDES = 1 + 6 * RH
ADDED = KT - 3
LAG = 3
LAYER_STEPS = 157
TWO_PI = 6.283185307179586
C1 = 6.28125
C2 = float(np.float32(TWO_PI - C1).view(np.uint32) & 0xFFFFF000)
C2 = float(np.array(int(C2), np.uint32).view(np.float32))
C3 = float(np.float32(TWO_PI - C1 - C2))
ROUND = 12582912.0
MASKED = -1e30

K_ID, K_COL = 0, P
K_DECAY = K_COL + 8
K_MASK = K_DECAY + RH * T
K_ALL = K_MASK + 2 * T


def constants():
    k = np.zeros((P, K_ALL), np.float32)
    k[:, K_ID:K_ID + P] = np.eye(P, dtype=np.float32)
    p = np.arange(P)
    for col, half in ((0, 64), (2, 32)):
        freq = (np.float32(1.0) / (np.float32(10000.0) ** (np.arange(0, 2 * half, 2, dtype=np.float32) / np.float32(2 * half)))).astype(np.float32)
        k[:, K_COL + col] = freq[p % half]
        k[:, K_COL + col + 1] = np.where(p % (2 * half) < half, -1.0, 1.0)
    k[:, K_COL + 4] = 1.0
    k[:, K_COL + 5] = np.pi / 2
    rel = np.arange(T)[None, :] - p[:, None]
    for h in range(RH):
        log_gamma = np.log1p(-(2.0 ** (-5.0 - h)))
        k[:, K_DECAY + h * T:K_DECAY + (h + 1) * T] = np.where(rel >= 0, np.exp(np.maximum(rel, 0) * log_gamma), 0.0) * P ** -0.5
    i, j = np.arange(P)[:, None] + P, np.arange(2 * P)[None, :]
    band = (i - j >= 0) & (i - j < P)
    for half in range(2):
        for b in range(2):
            seen = band & (j >= P) if half == b == 0 else band
            at = K_MASK + half * T + b * 2 * P
            k[:, at:at + 2 * P] = np.where(seen, 0.0, MASKED)
    return k


def decoder(nc, x, c, positions, norm_ffn1, norm_mix, norm_ffn2, final_norm, w_ada, b_ada,
            ffn1_w_up, ffn1_w_down, ffn2_w_up, ffn2_w_down, w_in, sinks, w_branch_ret,
            w_branch_swa, w_out, consts, out):
    F, R, I32 = mybir.dt.float32, mybir.dt.float32r, mybir.dt.int32
    ACT, ALU, AX = mybir.ActivationFunctionType, mybir.AluOpType, mybir.AxisListType
    ctx = ExitStack()
    with ctx:
        def sb(name, shape, dtype):
            return ctx.enter_context(nc.sbuf_tensor("sb_" + name, shape, dtype))

        def sem(name):
            return ctx.enter_context(nc.semaphore(name))

        XV = sb("x_or_values", [P, KT, T], F)
        Hhi, Hlo = sb("h_hi", [P, KT, T], R), sb("h_lo", [P, KT, T], R)
        Ahi, Alo = sb("a_hi", [P, 2 * KT, T], R), sb("a_lo", [P, 2 * KT, T], R)
        raw = [sb(f"raw{s}", [P, DOWN_UNIT], F) for s in range(2)]
        Whi = [sb(f"w_hi{s}", [P, DOWN_UNIT], R) for s in range(2)]
        Wlo = [sb(f"w_lo{s}", [P, DOWN_UNIT], R) for s in range(2)]
        K = sb("consts", [P, K_ALL], F)
        cos_r, sin_r = sb("cos_r", [P, T], F), sb("sin_r", [P, T], F)
        cos_s, sin_s = sb("cos_s", [P, T], F), sb("sin_s", [P, T], F)
        pos_i, pos_f = sb("pos_i", [P, T], I32), sb("pos_f", [P, T], F)
        vcols = sb("vector_cols", [P, 64 + 2 * MOD_TILES], F)
        c_act = sb("c_act", [P, KT], F)
        mod = sb("mod", [P, MOD_TILES], F)
        gain = sb("gain", [P, KT], F)
        half_gate = sb("half_gate", [P, KT], F)
        sink = sb("sinks", [P, DEPTH * QH], F)
        sm = sb("small", [P, 128], F)
        scratch = sb("scratch", [P, 12544], F)

        def view(at, n):
            return scratch[:, at:at + n]

        squares = view(0, 1024).rearrange("p (s t) -> p s t", s=2)
        square_sum = view(1024, T)
        merged_ret = view(0, 4096).rearrange("p (k t) -> p k t", t=T)
        ada_raw = [view(at, 1024).rearrange("p (k c) -> p k c", c=256) for at in (4096, 5120)]
        ada_acc = view(6144, 256)
        first_acc = [view(at, 256) for at in (6144, 6400, 6656, 6912, 7168)]
        side, work = view(6400, 512), view(6912, 512)
        tbuf = [view(7424 + 512 * s, 512) for s in range(3)]
        xtok = view(0, 4096).rearrange("p (t d) -> p t d", d=D)
        vec_rows = view(6400, 384).rearrange("p (a c) -> p a c", c=P)
        out_tok = view(0, 4096).rearrange("p (t d) -> p t d", d=D)
        first_raw = [[m.rearrange("p (k c) -> p k c", c=256) for m in two] for two in (
            [view(4096, 1024), view(5120, 1024)], [view(8448, 1024), view(9472, 1024)], [view(10496, 1024), view(11520, 1024)],
            [view(2048, 1024), view(3072, 1024)],
            [raw[0][:, 0:1024], raw[1][:, 0:1024]])]
        k_all = view(0, 1280).rearrange("p (v t) -> p v t", v=2)
        k_cur = view(1280, 640)
        sv_all = view(1920, 512).rearrange("p (t v d) -> p v t d", v=2, d=HD)
        sv_cur = view(2432, 256).rearrange("p (t d) -> p t d", d=HD)
        v_cur = view(2688, 1024).rearrange("p (t e) -> p t e", e=DV)
        sq = view(3712, 1024).rearrange("p (s t) -> p s t", s=2)
        rq, rk = view(4736, 512), view(5248, 512)
        ret_s = [view(7424 + 512 * s, 512) for s in range(2)]
        probs = [view(8448 + 1024 * s, 1024) for s in range(2)]
        probs_t = view(10496, 1024)
        silu_g = view(11520, 1024).rearrange("p (e t) -> p e t", e=2)
        V = XV[:, :, :].rearrange("p (h e) t -> p h (e t)", h=RH).rearrange("p h (t e) -> p h t e", e=DV)

        ident, ones = K[:, K_ID:K_ID + P], K[:, K_COL + 4:K_COL + 5]
        rstd = sm[:, 0:16]
        rs_t, rs_v = sm[:, 16:32], sm[:, 32:48]
        smax, neg_m, sink_d, row_sum, exp_sink, rden = (
            [sm[:, 48 + 8 * n + 4 * s:52 + 8 * n + 4 * s] for s in range(2)] for n in range(6))
        neg_mean = sm[:, 96:112]

        pA = [ctx.enter_context(nc.psum_tensor(f"ps_proj{s}", [P, T], F)) for s in range(2)]
        pM = ctx.enter_context(nc.psum_tensor("ps_mid", [P, 4, T], F))
        pO = ctx.enter_context(nc.psum_tensor("ps_o", [P, T], F))
        pS = ctx.enter_context(nc.psum_tensor("ps_small", [P, T], F))
        pC = pM[:, 3, 0:2]

        x_spill = nc.dram_tensor("x_spill", [P, KT * T], F, kind="Internal").ap()

        const_in, x_in, tables_in = sem("const_in"), sem("x_in"), sem("tables_in")
        landed = [sem("landed0"), sem("landed1")]
        hi_ready, lo_ready = sem("hi_ready"), sem("lo_ready")
        unit_done = sem("unit_done")
        bank_free = [sem("bank_free0"), sem("bank_free1")]
        first_in = [sem(f"first_in{q}") for q in range(FIRST_JOBS)]
        first_used, first_step, first_sum, first_col, first_mod = (
            sem(n) for n in ("first_used", "first_step", "first_sum", "first_col", "first_mod"))
        ada_in, ada_used, ada_step = [sem("ada_in0"), sem("ada_in1")], sem("ada_used"), sem("ada_step")
        ada_col, mod_done = sem("ada_col"), sem("mod_done")
        cols_ps, cols_done, c_done = sem("cols_ps"), sem("cols_done"), sem("c_done")
        xt_ps, xt_done = sem("xt_ps"), sem("xt_done")
        pos_done, ang_done_r, ang_done_s, tables_done = sem("pos_done"), sem("ang_done_r"), sem("ang_done_s"), sem("tables_done")
        sq_ready, sq_used, ss_ready, rstd_ready, rb_ready = sem("sq_ready"), sem("sq_used"), sem("ss_ready"), sem("rstd_ready"), sem("rb_ready")
        t_ready, split_hi, split_lo = sem("t_ready"), sem("split_hi"), sem("split_lo")
        act_hi, act_lo = sem("act_hi"), sem("act_lo")
        x_out, x_back = sem("x_out"), sem("x_back")
        v_ps, v_mean, v_done = sem("v_ps"), sem("v_mean"), sem("v_done")
        sv_done, k_zero, k_done = sem("sv_done"), sem("k_zero"), sem("k_done")
        swapped, rope_done = sem("swapped"), sem("rope_done")
        key_in, head_in = sem("key_in"), sem("head_in")
        scores, max_ready, exp_ready, p_ready = sem("scores"), sem("max_ready"), sem("exp_ready"), sem("p_ready")
        pt_ps, pt_act, pt_dve, o_ps, o_hi, o_done = (sem(n) for n in ("pt_ps", "pt_act", "pt_dve", "o_ps", "o_hi", "o_done"))
        st_ps, st_done, y_ps, ysq, y_free, var_ps = (sem(n) for n in ("st_ps", "st_done", "y_ps", "ysq", "y_free", "var_ps"))
        mg_ready, mg_hi, mg_lo = sem("mg_ready"), sem("mg_hi"), sem("mg_lo")
        y_out, o_tok, stored = sem("y_out"), sem("o_tok"), sem("stored")
        carrier = {"pool": sem("pool_carrier"), "dve": sem("dve_carrier")}
        dve_step, act_step, pool_step = sem("dve_step"), sem("act_step"), sem("pool_step")

        up_v = [w.rearrange("l (k p) (g m c) -> l g m p k c", p=P, g=2, c=P) for w in (ffn1_w_up, ffn2_w_up)]
        down_v = [w.rearrange("l (h k p) (m c) -> l h m p k c", p=P, h=2, c=P) for w in (ffn1_w_down, ffn2_w_down)]
        in_v = w_in.rearrange("l (k p) (m c) -> l m p k c", p=P, c=P)
        rv_v = w_in.rearrange("l (j k p) n -> l j p k n", p=P, k=2)
        sq_v = {n: w.rearrange("l (k p) (m c) -> l m p k c", p=P, c=P)
                for n, w in (("ret", w_branch_ret), ("swa", w_branch_swa), ("out", w_out))}
        ada_v = w_ada.rearrange("l (s k p) (j c) -> l j s p k c", p=P, s=2, c=256)

        class Steps:

            def __init__(self, eng, own):
                self.eng, self.sem, self.base, self.n, self.made = eng, own, 0, 0, 0

            def mark(self, ins):
                ins.then_inc(self.sem, 1)
                self.n += 1
                self.made += 1

            def wait(self):
                self.eng.wait_ge(self.sem, self.base + self.n)

            @contextmanager
            def loop(self, first, end, each):
                start, made = self.base + self.n, self.made
                with self.eng.Fori(first, end) as i:
                    self.base, self.n = start + (i - first) * each, 0
                    yield i
                    assert self.made - made == each, self.made - made
                self.made = made + (end - first) * each
                self.base, self.n = start + (end - first) * each, 0

        def pair_no(l, off):
            return l * LAYER_PAIRS + off

        def gated_no(l, off):
            return l * LAYER_GATED + (off if off < HEAD0 else off - UNGATED)

        def job_no(l, q):
            return l * JOBS + q - FIRST_JOBS

        NORM_SPLIT = {"ffn1": 0, "mix": KT, "ret": 2 * KT, "ffn2": 3 * KT}
        NORM_NO = {"ffn1": 0, "mix": 1, "ret": 2, "ffn2": 3}
        MOD_COL = {"ffn1": 0, "mix": 3 * KT, "ffn2": 6 * KT}
        GAIN_COL = {"ffn1": 8, "mix": 24, "ffn2": 40, "final": 56}
        FFN = (("ffn1", 0), ("ffn2", FFN2))

        block = ctx.enter_context(nc.Block())

        def angles(eng, st, col, n, ang, tmp):
            def op(out, in0, *a):
                st.mark(eng.tensor_scalar(out, in0, *a))
                st.wait()

            op(ang, pos_f[:, :], K[:, K_COL + col:K_COL + col + 1], None, ALU.mult)
            op(n, ang, 1.0 / TWO_PI, ROUND, ALU.mult, ALU.add)
            op(n, n, ROUND, None, ALU.subtract)
            for part in (C1, C2, C3):
                op(tmp, n, part, None, ALU.mult)
                st.mark(eng.tensor_tensor(ang, ang, tmp, ALU.subtract))
                st.wait()
            return eng.tensor_scalar(ang, ang, float(np.float32(-3.1415925)), float(np.float32(3.1415925)), ALU.max, ALU.min)

        @block.sync
        def _(sp):
            sp.dma_start(K[:, 0:K_DECAY], consts[:, 0:K_DECAY]).then_inc(const_in, 16)
            sp.dma_start(vec_rows[0:8, 0, :], c.rearrange("b (k p) -> (b k) p", p=P)).then_inc(const_in, 16)
            for n, w in enumerate((norm_ffn1, norm_mix, norm_ffn2)):
                sp.dma_start(vec_rows[8 + 16 * n:24 + 16 * n, 0, :], w.rearrange("l (k p) -> (l k) p", p=P)).then_inc(const_in, 16)
            sp.dma_start(vec_rows[56:64, 0, :], final_norm.rearrange("(k p) -> k p", p=P)).then_inc(const_in, 16)
            for l in range(DEPTH):
                sp.dma_start(vec_rows[0:MOD_TILES, 1 + l, :], b_ada[l].rearrange("(k p) -> k p", p=P)).then_inc(const_in, 16)
            sp.dma_start(pos_i[:, :], positions.broadcast_to([P, T])).then_inc(const_in, 16)
            sp.dma_start(xtok[:, :, :], x[0].rearrange("(t p) d -> p t d", p=P)).then_inc(x_in, 16)
            for q in range(FIRST_JOBS):
                if q == 3:
                    sp.wait_ge(xt_ps, KT)
                elif q == 5:
                    sp.wait_ge(first_used, 1)
                elif q > 5:
                    sp.wait_ge(first_sum, q - 5)
                for half in range(2):
                    sp.dma_start(first_raw[q % 5][half], ada_v[0, q, half]).then_inc(first_in[q], 16)

            def load(b, s, src, k=KT):
                sp.wait_ge(lo_ready, 2 * b + s + 1)
                sp.dma_start(raw[s][:, 0:k * P].rearrange("p (k c) -> p k c", k=src.shape[1]), src).then_inc(landed[s], 16)

            def ffn_loads(l, f, half):
                name, first = FFN[f]
                b0 = pair_no(l, first + half * HALF_PAIRS)

                def up(i, b):
                    for s in range(2):
                        load(b, s, up_v[f][l, s, HALF * half + i])

                if f or half:
                    up(0, b0)
                with sp.Fori(1, HALF) as i:
                    up(i, b0 + i)
                with sp.Fori(0, KT // 2) as j:
                    for s in range(2):
                        load(b0 + HALF + j, s, down_v[f][l, half, 2 * j + s], HALF)

            def tables():
                sp.dma_start(K[:, K_DECAY:], consts[:, K_DECAY:]).then_inc(tables_in, 16)
                sp.dma_start(sink[:, :], sinks.rearrange("l h -> (l h)").unsqueeze(0).broadcast_to([P, DEPTH * QH])).then_inc(tables_in, 16)

            tables()
            sp.wait_ge(first_sum, 3)
            with sp.Fori(0, DEPTH) as l:
                for s in range(2):
                    load(pair_no(l, 0), s, up_v[0][l, s, 0])
                ffn_loads(l, 0, 0)
                ffn_loads(l, 0, 1)
                for j in range(2 * V_PAIRS):
                    if j == 4:
                        sp.wait_ge(sq_ready, 3 * KT * l + 2 * KT)
                        sp.dma_start(x_spill, XV[:, :, :].rearrange("p k t -> p (k t)")).then_inc(x_out, 16)
                    at = RV_COL + T * (j // 4)
                    load(pair_no(l, MIX0 + j // 2), j % 2, rv_v[l, j % 4][:, :, at:at + T])
                load(pair_no(l, KV_PAIR), 0, in_v[l, SK])
                load(pair_no(l, KV_PAIR), 1, in_v[l, SV])
                with sp.Fori(0, RH) as i:
                    b = pair_no(l, HEAD0) + 3 * i
                    load(b, 0, in_v[l, SQ + 2 * i])
                    load(b, 1, in_v[l, SQ + 1 + 2 * i])
                    load(b + 1, 0, in_v[l, RQ + i])
                    load(b + 1, 1, in_v[l, RK + i])
                    load(b + 2, 0, in_v[l, RG + 2 * i])
                    load(b + 2, 1, in_v[l, RG + 1 + 2 * i])
                with sp.Fori(0, KT) as m:
                    load(pair_no(l, GATE_S0) + m, 0, in_v[l, GS + m])
                    load(pair_no(l, GATE_S0) + m, 1, sq_v["swa"][l, m])
                for first, end in ((0, 4), (4, KT)):
                    with sp.Fori(first, end) as m:
                        load(pair_no(l, GATE_R0) + m, 0, in_v[l, GR + m])
                        load(pair_no(l, GATE_R0) + m, 1, sq_v["ret"][l, m])
                    if first == 0:
                        sp.wait_ge(split_lo, LAYER_SPLITS * l + NORM_SPLIT["ffn2"])
                        sp.wait_ge(x_out, 16 * (l + 1))
                        sp.dma_start(XV[:, :, :].rearrange("p k t -> p (k t)"), x_spill).then_inc(x_back, 16)
                with sp.Fori(0, KT // 2) as j:
                    for s in range(2):
                        load(pair_no(l, OUT0) + j, s, sq_v["out"][l, 2 * j + s])
                ffn_loads(l, 1, 0)
                ffn_loads(l, 1, 1)
            for h in range(2):
                sp.wait_ge(o_tok, 4 * (h + 1))
                sp.dma_start(out[0].rearrange("(t p) d -> p t d", p=P)[:, :, 512 * h:512 * (h + 1)],
                             out_tok[:, :, 512 * h:512 * (h + 1)]).then_inc(stored, 16)
            sp.wait_ge(stored, 32)

        @block.gpsimd
        def _(pool):
            st = Steps(pool, pool_step)
            pool.wait_ge(const_in, 16 * 9)
            pool.tensor_copy(pos_f[:, :], pos_i[:, :]).then_inc(pos_done, 1)
            pool.wait_ge(pos_done, 1)
            angles(pool, st, 0, cos_r[:, :], sin_r[:, :], tbuf[0]).then_inc(ang_done_r, 1)

            def add_squares(no):
                for k in range(1, 1 + ADDED):
                    pool.wait_ge(sq_ready, KT * no + k + 1)
                    if k > 1:
                        pool.wait_ge(sq_used, ADDED * no + k - 1)
                    pool.sem_inc(carrier["pool"], 1)
                    pool.tensor_tensor(square_sum, square_sum, squares[:, k % 2, :], ALU.add).then_inc(sq_used, 1)

            add_squares(0)
            with pool.Fori(0, DEPTH) as l:
                add_squares(3 * l + 1)
                pool.wait_ge(ss_ready, 3 * l + 2)
                pool.sem_inc(carrier["pool"], 1)
                pool.memset(k_all[:, :, 0:P], 0.0).then_inc(k_zero, 1)
                pool.wait_ge(k_zero, l + 1)
                pool.wait_ge(v_done, 2 * TT * (l + 1))
                pool.wait_ge(sv_done, l + 1)
                pool.wait_ge(k_done, l + 1)
                pool.sem_inc(carrier["pool"], 1)
                for kv in range(2):
                    with pool.Fori(0, 2) as r:
                        pool.wait_ge(unit_done, 2 * pair_no(l, HEAD0) + 12 * kv + 6 * r + 2)
                        pool.sem_inc(carrier["pool"], 1)
                        pool.tensor_copy(k_cur, k_all[:, kv, :]).then_inc(key_in, 1)
                        pool.wait_ge(y_ps, RH * l + 2 * kv + r + 1)
                        pool.sem_inc(carrier["pool"], 1)
                        pool.tensor_copy(sv_cur, sv_all[:, kv])
                        pool.tensor_copy(v_cur, V[:, 2 * kv + r]).then_inc(head_in, 1)
                for n in range(2, 4):
                    add_squares(3 * l + n)

        @block.scalar
        def _(act):
            st = Steps(act, act_step)
            act.wait_ge(cols_done, 1)
            act.activation(c_act[:, :], vcols[:, 0:KT], ACT.Silu).then_inc(c_done, 1)

            def split_weights(b, s, n):
                act.wait_ge(landed[s], 16 * (b + 1))
                act.wait_ge(unit_done, 2 * b + s + 1)
                act.activation(Whi[s][:, 0:n], raw[s][:, 0:n], ACT.Copy).then_inc(hi_ready, 1)

            def square(no, k, s, ready, value):
                act.wait_ge(ready, value)
                if not isinstance(no, int):
                    act.wait_ge(ss_ready, no)
                if not isinstance(k, int) or k >= 3:
                    act.wait_ge(sq_used, ADDED * no + k - 2)
                to = square_sum if isinstance(k, int) and k == 0 else squares[:, s, :]
                act.activation(to, XV[:, k, :], ACT.Square).then_inc(sq_ready, 1)

            def load_job(l, q):
                for s in range(2):
                    act.wait_ge(ada_used, 2 * job_no(l, q) + s + 1)
                    act.dma_start(ada_raw[s], ada_v[l, q, s]).then_inc(ada_in[s], 16)

            def load_next_layers_job(l, n):
                with act.If(l < DEPTH - 1):
                    next_l = nc.s_assert_within(l + 1, 1, DEPTH - 1, skip_runtime_bounds_check_because="the last layer does not come here")
                    for s in range(2):
                        act.wait_ge(ada_used, 2 * job_no(l, JOBS + n) + s + 1)
                        act.dma_start(ada_raw[s], ada_v[next_l, n, s]).then_inc(ada_in[s], 16)

            def norm_hi(l, name):
                q = LAYER_SPLITS * l + NORM_SPLIT[name]
                for k in range(KT):
                    act.wait_ge(t_ready, q + k + 1)
                    shift = mod[:, MOD_COL[name] + k:MOD_COL[name] + k + 1]
                    act.activation(Hhi[:, k, :], tbuf[k % 3], ACT.Identity, bias=shift).then_inc(split_hi, 1)

            def ffn(l, f):
                name, first = FFN[f]
                for half in range(2):
                    b0, g0 = pair_no(l, first + half * HALF_PAIRS), gated_no(l, first + half * HALF_PAIRS)
                    a0 = FT * (2 * l + f) + HALF * half
                    q0 = FIRST_JOBS + HALF_JOBS * half

                    def up(i, n_next, load=None):
                        b, g = b0 + i, g0 + i
                        act.wait_ge(unit_done, 2 * b + 3)
                        act.wait_ge(bank_free[1], g + 1)
                        act.activation(side, pA[0][:, :], ACT.Silu).then_inc(bank_free[0], 1)
                        split_weights(b + 1, 0, n_next)
                        if load:
                            load(l, i)
                        split_weights(b + 1, 1, n_next)
                        act.wait_ge(bank_free[1], g + 2)
                        act.activation(Ahi[:, i, :], work, ACT.Copy).then_inc(act_hi, 1)

                    if f == 0:
                        with act.Fori(0, HALF - 1) as i:
                            up(i, UP_UNIT, lambda l, i: load_job(l, q0 + i))
                        up(HALF - 1, DOWN_UNIT, lambda l, i: load_job(l, q0 + i))
                    elif half == 0:
                        with act.Fori(0, FIRST_JOBS) as i:
                            up(i, UP_UNIT, load_next_layers_job)
                        with act.Fori(FIRST_JOBS, HALF - 1) as i:
                            up(i, UP_UNIT)
                        up(HALF - 1, DOWN_UNIT)
                    else:
                        with act.Fori(0, HALF - 1) as i:
                            up(i, UP_UNIT)
                        up(HALF - 1, DOWN_UNIT)

                    def down(j, n_next, load=None):
                        last = isinstance(j, int) and j > 0
                        for s in range(2):
                            if n_next and not (last and s):
                                split_weights(b0 + HALF + j + 1, s, n_next)
                            if half == 1:
                                square(3 * l + (3 if f else 1), 2 * j + s, s, bank_free[s], g0 + HALF + j + 2)
                            if n_next and last and s:
                                split_weights(b0 + HALF + j + 1, s, n_next)
                            if load and s == 0:
                                load(l, j)

                    next_job = (lambda l, j: load_job(l, q0 + HALF + j)) if f == 0 else None
                    down(0, DOWN_UNIT, next_job)
                    with act.Fori(1, KT // 2 - 1) as j:
                        down(j, DOWN_UNIT, next_job)
                    down(KT // 2 - 1, 0 if f == 1 and half == 1 else UP_UNIT)

            def swap(b, s, g, rope_no, ps, halves):
                act.wait_ge(unit_done, 2 * b + s + 3)
                act.wait_ge(rope_done, rope_no + 1)
                act.wait_ge(bank_free[1], g + 1)
                for at in range(0, P, 2 * halves):
                    act.activation(side[at:at + halves], ps[at + halves:at + 2 * halves, :], ACT.Copy)
                    last = act.activation(side[at + halves:at + 2 * halves], ps[at:at + halves, :], ACT.Copy)
                last.then_inc(swapped, 1)

            def exps(no, w):
                act.wait_ge(max_ready, no + 1)
                act.activation(exp_sink[w], sink_d[w], ACT.Exp)
                for n in range(4):
                    p = probs[w][:, 256 * n:256 * (n + 1)]
                    last = act.activation(p, p, ACT.Exp, bias=neg_m[w][:, n:n + 1], scale=HD ** -0.5,
                                          accum_out=row_sum[w][:, n:n + 1])
                last.then_inc(exp_ready, 1)

            def probs_out(no):
                act.wait_ge(pt_ps, 2 * no + 1)
                act.activation(probs_t[:, 0:T], pM[:, 2, :], ACT.Copy).then_inc(pt_act, 1)

            def swa_out(no, tile):
                act.wait_ge(o_ps, no + 1)
                act.activation(Ahi[:, KT + tile, :], pO[:, :], ACT.Copy).then_inc(o_hi, 1)

            def ret_hi(l, k):
                act.wait_ge(t_ready, LAYER_SPLITS * l + NORM_SPLIT["ret"] + k + 1)
                act.activation(Ahi[:, k, :], tbuf[0], ACT.Copy).then_inc(split_hi, 1)

            act.wait_ge(xt_ps, KT)
            for k in range(KT):
                square(0, k, k % 2, xt_done, k + 1)
            for n, (cos, sin, col, done) in enumerate(((cos_r, sin_r, 1, ang_done_r), (cos_s, sin_s, 3, ang_done_s))):
                act.wait_ge(done, 1)
                st.mark(act.activation(cos[:, :], sin[:, :], ACT.Abs))
                st.wait()
                act.activation(cos[:, :], cos[:, :], ACT.Sin, scale=-1.0, bias=K[:, K_COL + 5:K_COL + 6])
                act.activation(sin[:, :], sin[:, :], ACT.Sin, scale=K[:, K_COL + col:K_COL + col + 1]).then_inc(tables_done, 1)
            with act.Fori(0, DEPTH) as l:
                for s in range(2):
                    split_weights(pair_no(l, 0), s, UP_UNIT)
                norm_hi(l, "ffn1")
                ffn(l, 0)
                norm_hi(l, "mix")
                for p in range(V_PAIRS):
                    if p % 2 == 1:
                        split_weights(pair_no(l, MIX0 + p + 1), 0, UP_UNIT)
                        for tt in range(TT):
                            if tt == TT - 1:
                                split_weights(pair_no(l, MIX0 + p + 1), 1, UP_UNIT)
                            n = (p // 2) * TT + tt
                            act.wait_ge(v_mean, 2 * TT * l + n + 1)
                            act.wait_ge(x_out, 16 * (l + 1))
                            for h in range(2):
                                last = act.activation(V[:, 2 * (p // 2) + h, tt, :], pM[:, tt, DV * h:DV * (h + 1)],
                                                      ACT.Identity, bias=neg_mean[:, 2 * n + h:2 * n + h + 1])
                            last.then_inc(v_done, 1)
                    else:
                        for s in range(2):
                            split_weights(pair_no(l, MIX0 + p + 1), s, UP_UNIT)
                b, g = pair_no(l, KV_PAIR), gated_no(l, HEAD0)
                swap(b, 0, g, LAYER_ROPES * l, pS, HD // 2)
                split_weights(b + 1, 0, UP_UNIT)
                act.wait_ge(unit_done, 2 * b + 4)
                act.activation(sv_all.rearrange("p v t d -> p t v d"), pO[:, :].rearrange("p (t v d) -> p t v d", v=2, d=HD), ACT.Copy).then_inc(sv_done, 1)
                split_weights(b + 1, 1, UP_UNIT)
                def start_query(i, s):
                    b, g = pair_no(l, HEAD0) + 3 * i, gated_no(l, HEAD0) + 3 * i
                    swap(b, s, g, LAYER_ROPES * l + 1 + 4 * i + s, pA[s], HD // 2)
                    split_weights(b + 1, s, UP_UNIT)

                def middle(i):
                    b, g = pair_no(l, HEAD0) + 3 * i, gated_no(l, HEAD0) + 3 * i
                    rope0 = LAYER_ROPES * l + 1 + 4 * i
                    h0 = 4 * (RH * l + i)
                    exps(h0, 0)
                    swap(b + 1, 0, g + 1, rope0 + 2, pA[0], P // 2)
                    split_weights(b + 2, 0, UP_UNIT)
                    exps(h0 + 1, 1)
                    swap(b + 1, 1, g + 1, rope0 + 3, pA[1], P // 2)
                    split_weights(b + 2, 1, UP_UNIT)
                    probs_out(h0)
                    exps(h0 + 2, 0)
                    for s in range(2):
                        act.wait_ge(unit_done, 2 * (b + 2) + s + 3)
                        act.wait_ge(rope_done, rope0 + 4 + 1)
                        if s:
                            act.wait_ge(bank_free[0], g + 2 + 2)
                        act.activation(side, pA[s][:, :], ACT.Tanh, scale=0.5).then_inc(swapped, 1)
                        split_weights(b + 3, s, UP_UNIT)
                        if s == 0:
                            probs_out(h0 + 1)
                            exps(h0 + 3, 1)

                def tail(i, start):
                    h0 = 4 * (RH * l + i)
                    swa_out(2 * (RH * l + i), 2 * i)
                    probs_out(h0 + 2)
                    start(0)
                    probs_out(h0 + 3)
                    start(1)
                    swa_out(2 * (RH * l + i) + 1, 2 * i + 1)
                    act.wait_ge(y_ps, RH * l + i + 2)
                    for e in range(2):
                        act.activation(probs[1][:, T * e:T * (e + 1)], pM[:, 2 + e, :], ACT.Square).then_inc(ysq, 1)

                for s in range(2):
                    start_query(0, s)
                with act.Fori(0, RH - 1) as i:
                    middle(i)
                    tail(i, lambda s: start_query(i + 1, s))
                middle(RH - 1)
                tail(RH - 1, lambda s: None)
                with act.Fori(0, KT // 2) as j:
                    for s in range(2):
                        m = 2 * j + s
                        b, g = pair_no(l, GATE_S0) + m, gated_no(l, GATE_S0) + m
                        act.wait_ge(unit_done, 2 * b + 3)
                        act.wait_ge(bank_free[1], g + 1)
                        act.activation(side, pA[0][:, :], ACT.Tanh, scale=0.5).then_inc(bank_free[0], 1)
                        split_weights(b + 1, 0, UP_UNIT)
                        ret_hi(l, m)
                        split_weights(b + 1, 1, UP_UNIT)
                with act.Fori(0, KT) as m:
                    b, g = pair_no(l, GATE_R0) + m, gated_no(l, GATE_R0) + m
                    act.wait_ge(unit_done, 2 * b + 3)
                    act.wait_ge(bank_free[1], g + 1)
                    act.activation(side, pA[0][:, :], ACT.Tanh, scale=0.5).then_inc(bank_free[0], 1)
                    for s in range(2):
                        split_weights(b + 1, s, UP_UNIT)
                    act.wait_ge(mg_ready, KT * l + m + 1)
                    act.activation(Ahi[:, KT + m, :], work, ACT.Copy).then_inc(mg_hi, 1)

                def out(j):
                    b, g = pair_no(l, OUT0) + j, gated_no(l, OUT0) + j
                    split_weights(b + 1, 0, UP_UNIT)
                    square(3 * l + 2, 2 * j, 0, bank_free[0], g + 2)
                    if isinstance(j, int) and j > 0:
                        square(3 * l + 2, 2 * j + 1, 1, bank_free[1], g + 2)
                        split_weights(b + 1, 1, UP_UNIT)
                    else:
                        split_weights(b + 1, 1, UP_UNIT)
                        square(3 * l + 2, 2 * j + 1, 1, bank_free[1], g + 2)

                out(0)
                with act.Fori(1, KT // 2 - 1) as j:
                    out(j)
                out(KT // 2 - 1)
                norm_hi(l, "ffn2")
                ffn(l, 1)
            for k in range(KT):
                act.wait_ge(y_out, k + 1)
                act.activation(out_tok[:, :, P * k:P * (k + 1)], pA[k % 2][:, :].rearrange("p (t c) -> p t c", c=P),
                               ACT.Copy).then_inc(o_tok, 1)

        @block.vector
        def _(dve):
            st = Steps(dve, dve_step)
            dve.sem_inc(lo_ready, 2)
            for s in range(2):
                dve.sem_inc(bank_free[s], 1)
            for own in (rope_done, mod_done, o_done, act_lo, mg_lo):
                dve.sem_inc(own, 1)
            dve.sem_inc(ada_used, 2)
            dve.sem_inc(y_free, 2)
            dve.wait_ge(cols_ps, 1)
            dve.tensor_copy(vcols[:, :], pS[:, 0:64 + 2 * MOD_TILES]).then_inc(cols_done, 1)
            dve.wait_ge(pos_done, 1)
            angles(dve, st, 2, cos_s[:, :], sin_s[:, :], tbuf[1]).then_inc(ang_done_s, 1)
            for k in range(KT):
                dve.wait_ge(xt_ps, k + 1)
                dve.tensor_copy(XV[:, k, :], pA[k % 2][:, :]).then_inc(xt_done, 1)

            def split_weights(b, s, n):
                dve.wait_ge(hi_ready, 2 * b + s + 1)
                dve.tensor_tensor(Wlo[s][:, 0:n], raw[s][:, 0:n], Whi[s][:, 0:n].bitcast(F), ALU.subtract).then_inc(lo_ready, 1)

            def ada_sum_job(l, q):
                no = job_no(l, q)
                for k in range(KT):
                    s, col = k // 4, c_act[:, k:k + 1]
                    if k % 4 == 0:
                        dve.wait_ge(ada_in[s], 16 * (no + 1))
                    if k == 0:
                        ins = dve.tensor_scalar(ada_acc, ada_raw[0][:, 0, :], col, None, ALU.mult)
                    else:
                        ins = dve.scalar_tensor_tensor(ada_acc, ada_raw[s][:, k % 4, :], col, ada_acc, ALU.mult, ALU.add)
                    if k % 4 == 3:
                        ins.then_inc(ada_used, 1)
                        if s == 0:
                            dve.wait_ge(ada_used, 2 * no + 3)
                    else:
                        ins.then_inc(ada_step, 1)
                        dve.wait_ge(ada_step, 6 * no + k - s + 1)

            def ada_store_job(l, q, to, bias):
                dve.wait_ge(ada_col, job_no(l, q) + 1)
                dve.tensor_tensor(mod[:, bass.ds(2 * to, 2)], pC, vcols[:, bass.ds(64 + bias, 2)],
                                  ALU.add).then_inc(mod_done, 1)

            def rstd_of(n, scale, ready, value, last_scale=None):
                y, a, v = rstd[:, 0:n], rs_t[:, 0:n], rs_v[:, 0:n]
                dve.wait_ge(ready, value)
                chain = [
                    lambda: dve.tensor_scalar(v, pS[:, 0:n], scale, EPS, ALU.mult, ALU.add),
                    lambda: dve.tensor_scalar(y.bitcast(I32), v.bitcast(I32), 1, None, ALU.logical_shift_right),
                    lambda: dve.tensor_scalar(y.bitcast(I32), y.bitcast(I32), -1.0, float(0x5F3759DF), ALU.mult, ALU.add),
                ]
                for _ in range(3):
                    chain += [
                        lambda: dve.tensor_tensor(a, y, y, ALU.mult),
                        lambda: dve.scalar_tensor_tensor(a, a, -0.5, v, ALU.mult, ALU.mult),
                        lambda: dve.scalar_tensor_tensor(y, a, 1.5, y, ALU.add, ALU.mult),
                    ]
                if last_scale:
                    chain += [lambda: dve.tensor_scalar(y, y, last_scale, None, ALU.mult)]
                for op in chain[:-1]:
                    st.mark(op())
                    st.wait()
                chain[-1]().then_inc(rstd_ready, 1)

            def norm(l, name, next_pair=None):
                at = MOD_COL[name]
                gcol = GAIN_COL[name]
                if next_pair is not None:
                    split_weights(next_pair, 1, UP_UNIT)
                dve.wait_ge(mod_done, job_no(l, FIRST_JOBS if name == "ffn1" else JOBS) + 1)
                if name == "ffn1":
                    dve.wait_ge(first_mod, 1)
                    dve.wait_ge(ang_done_r, 1)
                st.mark(dve.scalar_tensor_tensor(gain[:, :], mod[:, at + KT:at + 2 * KT], 1.0,
                                                 vcols[:, bass.ds(gcol + KT * l, KT)], ALU.add, ALU.mult))
                no, q = 4 * l + NORM_NO[name], LAYER_SPLITS * l + NORM_SPLIT[name]
                st.wait()
                dve.wait_ge(rb_ready, no + 1)

                def lo(k):
                    dve.wait_ge(split_hi, q + k + 1)
                    dve.scalar_tensor_tensor(Hlo[:, k, :], tbuf[k % 3], mod[:, at + k:at + k + 1],
                                             Hhi[:, k, :].bitcast(F), ALU.add, ALU.subtract).then_inc(split_lo, 1)

                for k in range(KT):
                    if k >= 3:
                        dve.wait_ge(split_lo, q + k - 2)
                    dve.scalar_tensor_tensor(tbuf[k % 3], pO[:, :], gain[:, k:k + 1], XV[:, k, :],
                                             ALU.mult, ALU.mult).then_inc(t_ready, 1)
                    if k:
                        lo(k - 1)
                lo(KT - 1)

            def add_gated(s, g, b, m):
                dve.wait_ge(unit_done, 2 * b + s + 3)
                dve.scalar_tensor_tensor(XV[:, m, :], pA[s][:, :], half_gate[:, bass.ds(m, 1)], XV[:, m, :],
                                         ALU.mult, ALU.add).then_inc(bank_free[s], 1)

            def halve_gate(l, name):
                at = MOD_COL[name] + 2 * KT
                dve.wait_ge(mod_done, job_no(l, FIRST_JOBS + HALF - 1 if name == "ffn1" else JOBS) + 1)
                st.mark(dve.tensor_scalar(half_gate[:, :], mod[:, at:at + KT], 0.5, None, ALU.mult))
                st.wait()
                dve.sem_inc(carrier["dve"], 1)

            def ffn(l, f):
                name, first = FFN[f]
                for half in range(2):
                    b0, g0 = pair_no(l, first + half * HALF_PAIRS), gated_no(l, first + half * HALF_PAIRS)
                    a0 = FT * (2 * l + f) + HALF * half
                    q0 = FIRST_JOBS + HALF_JOBS * half

                    def up(i, n_next, jobs=None):
                        b, g = b0 + i, g0 + i
                        split_weights(b + 1, 0, n_next)
                        dve.wait_ge(unit_done, 2 * b + 4)
                        dve.wait_ge(bank_free[0], g + 2)
                        dve.wait_ge(act_lo, a0 + i + 1)
                        dve.tensor_tensor(work, side, pA[1][:, :], ALU.mult).then_inc(bank_free[1], 1)
                        split_weights(b + 1, 1, n_next)
                        dve.wait_ge(act_hi, a0 + i + 1)
                        dve.tensor_tensor(Alo[:, i, :], work, Ahi[:, i, :].bitcast(F), ALU.subtract).then_inc(act_lo, 1)
                        if jobs:
                            jobs(i)

                    def store_job(n):
                        ada_store_job(l, q0 + n, q0 + n, MOD_TILES * l + 2 * (q0 + n))

                    def both_jobs(n):
                        store_job(n - 1)
                        ada_sum_job(l, q0 + n)

                    def next_layers_jobs(n, store=True, add=True):
                        with dve.If(l < DEPTH - 1):
                            if store:
                                ada_store_job(l, JOBS + n - 1, n - 1, nc.s_assert_within(
                                    MOD_TILES * (l + 1) + 2 * (n - 1), MOD_TILES, MOD_TILES * DEPTH - 2,
                                    skip_runtime_bounds_check_because="the last layer does not come here"))
                            if add:
                                ada_sum_job(l, JOBS + n)

                    if f == 0:
                        up(0, UP_UNIT, lambda n: ada_sum_job(l, q0))
                        with st.loop(1, HALF - 1, 0) as i:
                            up(i, UP_UNIT, both_jobs)
                        up(HALF - 1, DOWN_UNIT, both_jobs)
                    elif half == 0:
                        up(0, UP_UNIT, lambda n: next_layers_jobs(n, store=False))
                        with st.loop(1, FIRST_JOBS, 0) as i:
                            up(i, UP_UNIT, next_layers_jobs)
                        up(FIRST_JOBS, UP_UNIT, lambda n: next_layers_jobs(n, add=False))
                        with st.loop(FIRST_JOBS + 1, HALF - 1, 0) as i:
                            up(i, UP_UNIT)
                        up(HALF - 1, DOWN_UNIT)
                    else:
                        with st.loop(0, HALF - 1, 0) as i:
                            up(i, UP_UNIT)
                        up(HALF - 1, DOWN_UNIT)
                    if half == 0:
                        halve_gate(l, name)

                    def down(j, n_next):
                        for s in range(2):
                            add_gated(s, g0 + HALF + j, b0 + HALF + j, 2 * j + s)
                            if n_next and not (half and s and isinstance(j, int)):
                                split_weights(b0 + HALF + j + 1, s, n_next)

                    with st.loop(0, KT // 2 - 1, 0) as j:
                        down(j, DOWN_UNIT)
                        if f == 0:
                            both_jobs(HALF + j)
                    down(KT // 2 - 1, 0 if f == 1 and half == 1 else UP_UNIT)
                    if half == 1:
                        if f == 1:
                            with dve.If(l < DEPTH - 1):
                                split_weights(pair_no(l + 1, 0), 0, UP_UNIT)
                        rstd_of(TT, 1.0 / D, ss_ready, 3 * l + (4 if f else 2))
                        if f == 1:
                            with dve.If(l < DEPTH - 1):
                                split_weights(pair_no(l + 1, 0), 1, UP_UNIT)
                    if f == 0:
                        store_job(HALF_JOBS - 1)

            def rope(no, side_no, ps, cos, sin, outs, s=None):
                dve.wait_ge(swapped, side_no + 1)
                dve.wait_ge(rope_done, no + 1)
                first = dve.tensor_tensor(work, ps[:, :], cos[:, :], ALU.mult)
                if s is None:
                    st.mark(first)
                else:
                    first.then_inc(bank_free[s], 1)
                st.mark(dve.tensor_tensor(side, side, sin[:, :], ALU.mult))
                st.wait()
                for to, p0, p1 in outs:
                    last = dve.tensor_tensor(to, work[p0:p1], side[p0:p1], ALU.add)
                last.then_inc(rope_done, 1)

            def maxima(no, l, i, t, half, w):
                dve.wait_ge(scores, no + 1)
                mask = K[:, K_MASK + T * half:K_MASK + T * (half + 1)]
                st.mark(dve.tensor_tensor(probs[w].rearrange("p (a t) -> p a t", a=2), pM[:, 0:2, :],
                                          mask.unsqueeze(1).broadcast_to([P, 2, T]), ALU.add))
                st.wait()
                st.mark(dve.reduce_max(smax[w], probs[w].rearrange("p (n k) -> p n k", n=4), AX.X))
                st.wait()
                neg_sink = sink[:, bass.ds(QH * l + 4 * i + 2 * t, 2)].unsqueeze(2).broadcast_to([P, 2, 2])

                def two(a):
                    return a.rearrange("p (a b) -> p a b", a=2)

                st.mark(dve.scalar_tensor_tensor(two(neg_m[w]), two(smax[w]), -(HD ** -0.5), neg_sink, ALU.mult, ALU.min))
                st.wait()
                dve.tensor_tensor(two(sink_d[w]), two(neg_m[w]), neg_sink, ALU.subtract).then_inc(max_ready, 1)

            def normalise(no, w):
                dve.wait_ge(exp_ready, no + 1)
                st.mark(dve.tensor_tensor(rden[w], row_sum[w], exp_sink[w], ALU.add))
                st.wait()
                st.mark(dve.reciprocal(rden[w], rden[w]))
                st.wait()
                for n in range(4):
                    p = probs[w][:, 256 * n:256 * (n + 1)]
                    last = dve.tensor_scalar(p, p, rden[w][:, n:n + 1], None, ALU.mult)
                last.then_inc(p_ready, 1)

            def probs_out(no):
                dve.wait_ge(pt_ps, 2 * no + 2)
                dve.tensor_copy(probs_t[:, T:2 * T], pM[:, 3, :]).then_inc(pt_dve, 1)

            def swa_out(no, tile):
                dve.wait_ge(o_hi, no + 1)
                dve.tensor_tensor(Alo[:, KT + tile, :], pO[:, :], Ahi[:, KT + tile, :].bitcast(F), ALU.subtract).then_inc(o_done, 1)

            dve.wait_ge(c_done, 1)
            made, step = 0, {}
            for jobs in (DVE_JOBS[0:2], DVE_JOBS[2:4], DVE_JOBS[4:]):
                if jobs == DVE_JOBS[4:]:
                    rstd_of(TT, 1.0 / D, ss_ready, 1)
                for q in jobs:
                    dve.wait_ge(first_in[q], 32)
                for k in range(KT):
                    for q in jobs:
                        acc, col, tile = first_acc[DVE_JOBS.index(q)], c_act[:, k:k + 1], first_raw[q % 5][k // 4][:, k % 4, :]
                        if k == 0:
                            ins = dve.tensor_scalar(acc, tile, col, None, ALU.mult)
                        else:
                            dve.wait_ge(first_step, step[q])
                            ins = dve.scalar_tensor_tensor(acc, tile, col, acc, ALU.mult, ALU.add)
                        if k < KT - 1:
                            ins.then_inc(first_step, 1)
                            made += 1
                            step[q] = made
                        else:
                            ins.then_inc(first_sum, 1)
            for s in range(2):
                split_weights(0, s, UP_UNIT)
            dve.wait_ge(first_col, 1)
            dve.tensor_tensor(mod[:, 0:2 * FIRST_JOBS], pM[:, 3, 0:2 * FIRST_JOBS], vcols[:, 64:64 + 2 * FIRST_JOBS],
                              ALU.add).then_inc(first_mod, 1)
            dve.wait_ge(tables_in, 32)
            st.mark(dve.tensor_scalar(sink[:, :], sink[:, :], -1.0, None, ALU.mult))
            st.wait()
            with st.loop(0, DEPTH, LAYER_STEPS) as l:
                norm(l, "ffn1")
                ffn(l, 0)
                norm(l, "mix", pair_no(l, MIX0))
                for p in range(V_PAIRS):
                    split_weights(pair_no(l, MIX0 + p + 1), 0, UP_UNIT)
                    if p % 2 == 0:
                        split_weights(pair_no(l, MIX0 + p + 1), 1, UP_UNIT)
                    else:
                        for tt in range(TT):
                            if tt == TT - 1:
                                split_weights(pair_no(l, MIX0 + p + 1), 1, UP_UNIT)
                            n = (p // 2) * TT + tt
                            m = neg_mean[:, 2 * n:2 * n + 2]
                            if tt < TT - 1:
                                dve.wait_ge(v_ps, 2 * (TT - 1) * l + (TT - 1) * (p // 2) + tt + 1)
                            else:
                                dve.wait_ge(unit_done, 2 * pair_no(l, MIX0 + p) + 4)
                            st.mark(dve.reduce_sum(m, pM[:, tt, :].rearrange("p (h e) -> p h e", h=2), AX.X))
                            st.wait()
                            dve.tensor_scalar(m, m, -1.0 / DV, None, ALU.mult).then_inc(v_mean, 1)
                b = pair_no(l, KV_PAIR)
                dve.wait_ge(tables_done, 2)
                dve.wait_ge(k_zero, l + 1)
                rope(LAYER_ROPES * l, LAYER_SIDES * l, pS, cos_s, sin_s,
                     [(k_all[64 * h:64 * (h + 1), v, P:], 64 * v, 64 * (v + 1)) for v in range(2) for h in range(2)])
                dve.wait_ge(rope_done, LAYER_ROPES * l + 2)
                dve.sem_inc(k_done, 1)
                for s in range(2):
                    split_weights(b + 1, s, UP_UNIT)
                def numbers(i):
                    return (pair_no(l, HEAD0) + 3 * i, LAYER_SIDES * l + 1 + 6 * i, LAYER_ROPES * l + 1 + 4 * i, RH * l + i)

                def start_query(i, s):
                    b, side0, rope0, n0 = numbers(i)
                    rope(rope0 + s, side0 + s, pA[s], cos_s, sin_s, [(sq[:, s, :], 0, P)], s)

                def middle(i):
                    b, side0, rope0, n0 = numbers(i)
                    h0 = 4 * n0

                    def retention_rope(n, tile):
                        rope(rope0 + 2 + n, side0 + 2 + n, pA[n], cos_r, sin_r, [(tile, 0, P)], n)
                        split_weights(b + 2, n, UP_UNIT)

                    def retention_gate(n):
                        dve.wait_ge(swapped, side0 + 4 + n + 1)
                        dve.scalar_tensor_tensor(silu_g[:, n, :], side, 1.0, pA[n][:, :], ALU.add, ALU.mult).then_inc(bank_free[n], 1)
                        split_weights(b + 3, n, UP_UNIT)

                    maxima(h0, l, i, 0, 0, 0)
                    retention_rope(0, rq)
                    normalise(h0, 0)
                    maxima(h0 + 1, l, i, 0, 1, 1)
                    normalise(h0 + 1, 1)
                    retention_rope(1, rk)
                    probs_out(h0)
                    maxima(h0 + 2, l, i, 1, 0, 0)
                    normalise(h0 + 2, 0)
                    retention_gate(0)
                    probs_out(h0 + 1)
                    maxima(h0 + 3, l, i, 1, 1, 1)
                    retention_gate(1)
                    normalise(h0 + 3, 1)

                def tail(i, next_head):
                    b, side0, rope0, n0 = numbers(i)
                    h0 = 4 * n0

                    def decay(n):
                        w = T - P * n
                        dve.wait_ge(st_ps, TT * n0 + n + 1)
                        dve.tensor_tensor(ret_s[n % 2][:, 0:w], pM[:, n % 2, 0:w], K[:, bass.ds(K_DECAY + T * i, w)],
                                          ALU.mult).then_inc(st_done, 1)

                    swa_out(2 * n0, 2 * i)
                    probs_out(h0 + 2)
                    decay(0)
                    decay(1)
                    if next_head:
                        start_query(i + 1, 0)
                        split_weights(b + 4, 0, UP_UNIT)
                    probs_out(h0 + 3)
                    if next_head:
                        start_query(i + 1, 1)
                    swa_out(2 * n0 + 1, 2 * i + 1)
                    decay(2)
                    decay(3)
                    if next_head:
                        split_weights(b + 4, 1, UP_UNIT)
                    for e in range(2):
                        dve.wait_ge(ysq, 2 * n0 + e + 1)
                        dve.tensor_tensor(XV[:, 2 * i + e, :], pM[:, 2 + e, :], silu_g[:, e, :], ALU.mult).then_inc(y_free, 1)

                for s in range(2):
                    start_query(0, s)
                    split_weights(b + 2, s, UP_UNIT)
                with st.loop(0, RH - 1, 4 + 4 * 5) as i:
                    middle(i)
                    tail(i, True)
                middle(RH - 1)
                tail(RH - 1, False)
                rstd_of(TT * RH, 1.0 / DV, var_ps, RH * (l + 1), 0.5)
                with st.loop(0, KT // 2, 0) as j:
                    for s in range(2):
                        m = 2 * j + s
                        b, g = pair_no(l, GATE_S0) + m, gated_no(l, GATE_S0) + m
                        q = LAYER_SPLITS * l + NORM_SPLIT["ret"] + m
                        split_weights(b + 1, 0, UP_UNIT)
                        dve.wait_ge(bank_free[0], g + 2)
                        dve.wait_ge(unit_done, 2 * b + 4)
                        dve.scalar_tensor_tensor(merged_ret[:, m, :], side, 1.0, pA[1][:, :], ALU.add, ALU.mult).then_inc(bank_free[1], 1)
                        dve.wait_ge(rb_ready, 4 * l + 3)
                        dve.wait_ge(split_lo, q)
                        dve.tensor_tensor(tbuf[0], XV[:, m, :], pM[:, bass.ds(j, 1), :].rearrange("p a t -> p (a t)"), ALU.mult).then_inc(t_ready, 1)
                        split_weights(b + 1, 1, UP_UNIT)
                        dve.wait_ge(split_hi, q + 1)
                        dve.tensor_tensor(Alo[:, m, :], tbuf[0], Ahi[:, m, :].bitcast(F), ALU.subtract).then_inc(split_lo, 1)
                with st.loop(0, KT, 0) as m:
                    b, g = pair_no(l, GATE_R0) + m, gated_no(l, GATE_R0) + m
                    split_weights(b + 1, 0, UP_UNIT)
                    dve.wait_ge(bank_free[0], g + 2)
                    dve.wait_ge(unit_done, 2 * b + 4)
                    dve.wait_ge(mg_lo, KT * l + m + 1)
                    dve.scalar_tensor_tensor(work, side, 1.0, pA[1][:, :], ALU.add, ALU.mult).then_inc(bank_free[1], 1)
                    dve.wait_ge(bank_free[1], g + 2)
                    dve.tensor_tensor(work, work, merged_ret[:, m, :], ALU.add).then_inc(mg_ready, 1)
                    split_weights(b + 1, 1, UP_UNIT)
                    dve.wait_ge(mg_hi, KT * l + m + 1)
                    dve.tensor_tensor(Alo[:, KT + m, :], work, Ahi[:, KT + m, :].bitcast(F), ALU.subtract).then_inc(mg_lo, 1)
                dve.wait_ge(x_back, 16 * (l + 1))
                halve_gate(l, "mix")
                with st.loop(0, KT // 2 - 1, 0) as j:
                    b, g = pair_no(l, OUT0) + j, gated_no(l, OUT0) + j
                    for s in range(2):
                        add_gated(s, g, b, 2 * j + s)
                        split_weights(b + 1, s, UP_UNIT)
                b, g, j = pair_no(l, OUT0) + KT // 2 - 1, gated_no(l, OUT0) + KT // 2 - 1, KT // 2 - 1
                add_gated(0, g, b, 2 * j)
                split_weights(b + 1, 0, UP_UNIT)
                add_gated(1, g, b, 2 * j + 1)
                rstd_of(TT, 1.0 / D, ss_ready, 3 * l + 3)
                norm(l, "ffn2", pair_no(l, FFN2))
                ffn(l, 1)
            dve.wait_ge(rb_ready, 4 * DEPTH + 1)
            for k in range(KT):
                if k >= 2:
                    dve.wait_ge(y_out, k - 1)
                g = vcols[:, GAIN_COL["final"] + k:GAIN_COL["final"] + k + 1]
                dve.scalar_tensor_tensor(tbuf[k % 2], pO[:, :], g, XV[:, k, :], ALU.mult, ALU.mult).then_inc(t_ready, 1)

        @block.tensor
        def _(pe):
            pe.sem_inc(unit_done, 2)
            pe.sem_inc(y_ps, 1)
            pe.wait_ge(const_in, 16 * 9)
            pe.transpose(pS[:, 0:64], vec_rows[0:64, 0, :], ident[0:64, 0:64])
            for n in range(DEPTH):
                last = pe.transpose(pS[:, 64 + MOD_TILES * n:64 + MOD_TILES * (n + 1)], vec_rows[0:MOD_TILES, 1 + n, :],
                                    ident[0:MOD_TILES, 0:MOD_TILES])
            last.then_inc(cols_ps, 1)
            pe.wait_ge(x_in, 16)
            for k in range(KT):
                if k >= 2:
                    pe.wait_ge(xt_done, k - 1)
                for t in range(TT):
                    last = pe.transpose(pA[k % 2][:, P * t:P * (t + 1)], xtok[:, t, P * k:P * (k + 1)], ident)
                last.then_inc(xt_ps, 1)

            def sum_squares(no, part):
                if part == 0:
                    pe.wait_ge(sq_used, ADDED * (no + 1))
                else:
                    pe.wait_ge(sq_ready, KT * no + KT - 2 + part)
                tile = (square_sum, squares[:, 0, :], squares[:, 1, :])[part]
                for t in range(TT):
                    ins = pe.matmul(pS[:, t:t + 1], tile[:, P * t:P * (t + 1)], ones,
                                    start=(part == t == 0), stop=(part == 2), skip_group_check=True)
                if part == 2:
                    ins.then_inc(ss_ready, 1)

            def first_job(q):
                pe.wait_ge(c_done, 1)
                pe.wait_ge(first_in[q], 32)
                for k in range(KT):
                    for half in range(2):
                        last = pe.matmul(pM[:, 3, 2 * q + half:2 * q + half + 1],
                                         first_raw[q % 5][k // 4][:, k % 4, P * half:P * (half + 1)], c_act[:, k:k + 1],
                                         start=(q == k == half == 0), stop=(k == KT - 1), skip_group_check=True)
                last.then_inc(first_used, 1)

            def first_columns(n):
                pe.wait_ge(first_sum, n + 1)
                at = 2 * DVE_JOBS[n]
                for half in range(2):
                    last = pe.matmul(pM[:, 3, at + half:at + half + 1], first_acc[n][:, P * half:P * (half + 1)],
                                     ones, start=False, stop=True, skip_group_check=True)
                return last

            for q in PE_JOBS[0:2]:
                first_job(q)
            for n in range(2):
                first_columns(n)
            for part in range(3):
                sum_squares(0, part)
            first_job(PE_JOBS[2])
            for n in range(2, 4):
                first_columns(n)

            def product(bank, s, k, hi, lo, first, last):
                w = slice(P * k, P * (k + 1))
                pe.matmul(bank, Whi[s][:, w], hi, start=first, stop=False)
                pe.matmul(bank, Whi[s][:, w], lo, start=False, stop=False)
                return pe.matmul(bank, Wlo[s][:, w], hi, start=False, stop=last)

            def h_tile(k):
                return Hhi[:, k, :], Hlo[:, k, :]

            def a_tile(k):
                return Ahi[:, k, :], Alo[:, k, :]

            def start_unit(b, g, s):
                pe.wait_ge(lo_ready, 2 * b + s + 3)
                pe.wait_ge(bank_free[s], g + 1)

            def unit(b, g, s, tiles, at=0, n=KT, waits={}):
                start_unit(b, g, s)
                for k in range(n):
                    if k in waits:
                        pe.wait_ge(*waits[k])
                    last = product(pA[s][:, :], s, k, *tiles(at + k), k == 0, k == n - 1)
                last.then_inc(unit_done, 1)

            def ada_job(l, q):
                pe.wait_ge(ada_used, 2 * job_no(l, q) + 4)
                pe.wait_ge(mod_done, job_no(l, q) + 1)
                for n in range(2):
                    last = pe.matmul(pC[:, n:n + 1], ada_acc[:, P * n:P * (n + 1)], ones, start=True, stop=True)
                last.then_inc(ada_col, 1)

            def spread_rstd(no, bank, at):
                pe.wait_ge(rstd_ready, no + 1)
                for t in range(TT):
                    last = pe.matmul(bank[:, P * t:P * (t + 1)], rstd[:, at + t:at + t + 1].broadcast_to([P, P]), ident,
                                     start=True, stop=True)
                return last

            spread_rstd(0, pO, 0).then_inc(rb_ready, 1)
            first_columns(4).then_inc(first_col, 1)

            def add_pairs(no, pair):
                with pe.Fori(0, KT // 2 - 1) as j:
                    pair(j, lambda: None)
                pair(KT // 2 - 1, lambda: sum_squares(no, 0))
                for part in (1, 2):
                    sum_squares(no, part)

            def ffn(l, f):
                name, first = FFN[f]
                for half in range(2):
                    b0, g0 = pair_no(l, first + half * HALF_PAIRS), gated_no(l, first + half * HALF_PAIRS)
                    a0 = FT * (2 * l + f) + HALF * half
                    q0 = FIRST_JOBS + HALF_JOBS * half
                    if half == 0:
                        for s in range(2):
                            start_unit(b0, g0, s)
                        for k in range(KT + LAG):
                            for s, kk in ((0, k), (1, k - LAG)):
                                if not 0 <= kk < KT:
                                    continue
                                if s == 0:
                                    pe.wait_ge(split_lo, LAYER_SPLITS * l + NORM_SPLIT[name] + k + 1)
                                last = product(pA[s][:, :], s, kk, *h_tile(kk), kk == 0, kk == KT - 1)
                                if kk == KT - 1:
                                    last.then_inc(unit_done, 1)
                    else:
                        for s in range(2):
                            unit(b0, g0, s, h_tile)
                    with pe.Fori(1, FIRST_JOBS + 1 if f and half == 0 else HALF) as i:
                        for s in range(2):
                            unit(b0 + i, g0 + i, s, h_tile)
                        if f == 0:
                            ada_job(l, q0 + i - 1)
                        elif half == 0:
                            with pe.If(l < DEPTH - 1):
                                ada_job(l, JOBS + i - 1)
                    if f and half == 0:
                        with pe.Fori(FIRST_JOBS + 1, HALF) as i:
                            for s in range(2):
                                unit(b0 + i, g0 + i, s, h_tile)

                    def down(j, between):
                        for s in range(2):
                            unit(b0 + HALF + j, g0 + HALF + j, s, a_tile, 0, HALF,
                                 {0: (act_lo, a0 + HALF), HALF - 1: (act_lo, a0 + HALF + 1)})
                            if s == 0:
                                between()
                        if f == 0:
                            ada_job(l, q0 + HALF - 1 + j)

                    if half == 0:
                        with pe.Fori(0, KT // 2) as j:
                            down(j, lambda: None)
                    else:
                        add_pairs(3 * l + (3 if f else 1), down)
                        spread_rstd(4 * l + (4 if f else 1), pO, 0).then_inc(rb_ready, 1)

            def swa_scores(no, t, half):
                for n in range(2):
                    blk = 2 * half + n
                    for a in range(2):
                        p = slice(HD * a, HD * (a + 1))
                        last = pe.matmul(pM[:, a, 256 * n:256 * (n + 1)], sq[p, t, P * blk:P * (blk + 1)],
                                         k_cur[p, P * blk:P * (blk + 2)], start=True, stop=True)
                last.then_inc(scores, 1)

            def swa_transposes(no, w):
                pe.wait_ge(p_ready, no + 1)
                for a in range(2):
                    for n in range(4):
                        last = pe.transpose(pM[:, 2 + a, P * n:P * (n + 1)], probs[w][:, T * a + P * n:T * a + P * (n + 1)], ident)
                    last.then_inc(pt_ps, 1)

            def swa_values(no, half):
                pe.wait_ge(pt_act, no + 1)
                pe.wait_ge(pt_dve, no + 1)
                for n in range(2):
                    blk = 2 * half + n
                    for kt in range(0 if blk else 1, 2):
                        for a in range(2):
                            at = T * a + 256 * n + P * kt
                            last = pe.matmul(pO[HD * a:HD * (a + 1), P * blk:P * (blk + 1)], sv_cur[:, blk - 1 + kt, :],
                                             probs_t[:, at:at + P], start=(kt == (0 if blk else 1)), stop=(kt == 1))
                return last

            with pe.Fori(0, DEPTH) as l:
                ffn(l, 0)
                for j in range(2 * V_PAIRS):
                    b, s = pair_no(l, MIX0 + j // 2), j % 2
                    pe.wait_ge(lo_ready, 2 * b + s + 3)
                    for t in range(TT):
                        if j == 4:
                            pe.wait_ge(v_done, 2 * TT * l + t + 1)
                        for kk in range(2):
                            k = 2 * (j % 4) + kk
                            if j < 4 and t == 0:
                                pe.wait_ge(split_lo, LAYER_SPLITS * l + NORM_SPLIT["mix"] + k + 1)
                            w, tok = slice(T * kk, T * (kk + 1)), slice(P * t, P * (t + 1))
                            pe.matmul(pM[:, t, :], Hhi[:, k, tok], Whi[s][:, w], start=(k == 0), stop=False)
                            pe.matmul(pM[:, t, :], Hhi[:, k, tok], Wlo[s][:, w], start=False, stop=False)
                            last = pe.matmul(pM[:, t, :], Hlo[:, k, tok], Whi[s][:, w], start=False, stop=(k == KT - 1))
                        if j % 4 == 3 and t < TT - 1:
                            last.then_inc(v_ps, 1)
                    last.then_inc(unit_done, 1)
                b = pair_no(l, KV_PAIR)
                pe.wait_ge(lo_ready, 2 * b + 3)
                for k in range(KT):
                    last = product(pS[:, :], 0, k, *h_tile(k), k == 0, k == KT - 1)
                last.then_inc(unit_done, 1)
                pe.wait_ge(lo_ready, 2 * b + 4)
                for t in range(TT):
                    for k in range(KT):
                        w, tok = slice(P * k, P * (k + 1)), slice(P * t, P * (t + 1))
                        o = pO[:, P * t:P * (t + 1)]
                        pe.matmul(o, Hhi[:, k, tok], Whi[1][:, w], start=(k == 0), stop=False)
                        pe.matmul(o, Hhi[:, k, tok], Wlo[1][:, w], start=False, stop=False)
                        last = pe.matmul(o, Hlo[:, k, tok], Whi[1][:, w], start=False, stop=(k == KT - 1))
                last.then_inc(unit_done, 1)
                def numbers(i):
                    return (pair_no(l, HEAD0) + 3 * i, gated_no(l, HEAD0) + 3 * i, LAYER_ROPES * l + 1 + 4 * i, RH * l + i)

                def start_attention(i):
                    b, g, rope0, n0 = numbers(i)
                    pe.wait_ge(key_in, n0 + 1)
                    pe.wait_ge(rope_done, rope0 + 2)
                    swa_scores(4 * n0, 0, 0)
                    unit(b + 1, g + 1, 0, h_tile)

                def middle(i):
                    b, g, rope0, n0 = numbers(i)
                    h0, o0 = 4 * n0, 2 * n0
                    pe.wait_ge(max_ready, h0 + 1)
                    swa_scores(h0 + 1, 0, 1)
                    unit(b + 1, g + 1, 1, h_tile)
                    pe.wait_ge(y_free, 2 * n0 + 2)
                    swa_transposes(h0, 0)
                    pe.wait_ge(rope_done, rope0 + 3)
                    pe.wait_ge(max_ready, h0 + 2)
                    swa_scores(h0 + 2, 1, 0)
                    unit(b + 2, g + 2, 0, h_tile)
                    pe.wait_ge(o_done, o0 + 1)
                    pe.wait_ge(head_in, n0 + 1)
                    swa_values(h0, 0)
                    swa_transposes(h0 + 1, 1)
                    pe.wait_ge(max_ready, h0 + 3)
                    swa_scores(h0 + 3, 1, 1)
                    unit(b + 2, g + 2, 1, h_tile)

                def tail(i, unit_0, unit_1):
                    b, g, rope0, n0 = numbers(i)
                    h0, o0 = 4 * n0, 2 * n0

                    def ret_scores(n):
                        pe.matmul(pM[:, n % 2, 0:T - P * n], rk[:, P * n:P * (n + 1)], rq[:, P * n:T],
                                  start=True, stop=True).then_inc(st_ps, 1)

                    def ret_values(n):
                        pe.wait_ge(st_done, TT * n0 + n + 1)
                        for e in range(2):
                            last = pe.matmul(pM[:, 2 + e, P * n:T], v_cur[:, n, P * e:P * (e + 1)], ret_s[n % 2][:, 0:T - P * n],
                                             start=(n == 0), stop=(n == TT - 1))
                        return last

                    swa_values(h0 + 1, 1).then_inc(o_ps, 1)
                    swa_transposes(h0 + 2, 0)
                    pe.wait_ge(max_ready, h0 + 4)
                    pe.wait_ge(rope_done, rope0 + 5)
                    ret_scores(0)
                    ret_scores(1)
                    unit_0()
                    pe.wait_ge(o_done, o0 + 2)
                    swa_values(h0 + 2, 0)
                    swa_transposes(h0 + 3, 1)
                    unit_1()
                    swa_values(h0 + 3, 1).then_inc(o_ps, 1)
                    ret_values(0)
                    ret_scores(2)
                    ret_values(1)
                    ret_scores(3)
                    ret_values(2)
                    ret_values(3).then_inc(y_ps, 1)

                def variance(i):
                    n0 = RH * l + i
                    pe.wait_ge(ysq, 2 * n0 + 2)
                    for t in range(TT):
                        for e in range(2):
                            last = pe.matmul(pS[:, bass.ds(TT * i + t, 1)], probs[1][:, T * e + P * t:T * e + P * (t + 1)], ones,
                                             start=(e == 0), stop=(e == 1))
                    last.then_inc(var_ps, 1)

                for s in range(2):
                    unit(b + 1, gated_no(l, HEAD0), s, h_tile)
                start_attention(0)
                with pe.Fori(0, RH - 1) as i:
                    b, g, rope0, n0 = numbers(i + 1)
                    middle(i)
                    tail(i, lambda: unit(b, g, 0, h_tile), lambda: unit(b, g, 1, h_tile))
                    start_attention(i + 1)
                    variance(i)
                middle(RH - 1)
                b, g = pair_no(l, GATE_S0), gated_no(l, GATE_S0)
                tail(RH - 1, lambda: unit(b, g, 0, h_tile), lambda: None)
                variance(RH - 1)
                unit(b, g, 1, a_tile, KT, KT, {0: (o_done, 2 * RH * (l + 1) + 1)})
                pe.wait_ge(y_free, 2 * RH * (l + 1) + 2)
                for h in range(RH):
                    last = spread_rstd(4 * l + 2, pM[:, h, :], TT * h)
                last.then_inc(rb_ready, 1)
                with pe.Fori(1, KT) as m:
                    unit(b + m, g + m, 0, h_tile)
                    unit(b + m, g + m, 1, a_tile, KT)
                b, g = pair_no(l, GATE_R0), gated_no(l, GATE_R0)
                with pe.Fori(0, KT) as m:
                    unit(b + m, g + m, 0, h_tile)
                    unit(b + m, g + m, 1, a_tile, 0, KT, {0: (split_lo, LAYER_SPLITS * l + NORM_SPLIT["ffn2"])})
                b, g = pair_no(l, OUT0), gated_no(l, OUT0)

                def out(j, between):
                    for s in range(2):
                        unit(b + j, g + j, s, a_tile, KT, KT, {0: (mg_lo, KT * (l + 1)), KT - 1: (mg_lo, KT * (l + 1) + 1)})
                        if s == 0:
                            between()

                add_pairs(3 * l + 2, out)
                spread_rstd(4 * l + 3, pO, 0).then_inc(rb_ready, 1)
                ffn(l, 1)
            for k in range(KT):
                pe.wait_ge(t_ready, LAYER_SPLITS * DEPTH + k + 1)
                if k >= 2:
                    pe.wait_ge(o_tok, k - 1)
                for t in range(TT):
                    last = pe.transpose(pA[k % 2][:, P * t:P * (t + 1)], tbuf[k % 2][:, P * t:P * (t + 1)], ident)
                last.then_inc(y_out, 1)


_INS = ['x', 'c', 'positions', 'norm_ffn1', 'norm_mix', 'norm_ffn2', 'final_norm', 'w_ada', 'b_ada',
        'ffn1_w_up', 'ffn1_w_down', 'ffn2_w_up', 'ffn2_w_down', 'w_in', 'sinks', 'w_branch_ret',
        'w_branch_swa', 'w_out']


def kernel(**inputs):
    import concourse.bacc as bacc
    from concourse.bass_utils import run_bass_kernel_spmd

    nc = bacc.Bacc("TRN2", target_bir_lowering=False, num_devices=1, dynamic_dma_scratch_size=1024)
    arrays = {f"in_{n}": np.ascontiguousarray(inputs[n]) for n in _INS}
    arrays["in_consts"] = constants()
    args = [nc.dram_tensor(n, a.shape, mybir.dt.from_np(a.dtype), kind="ExternalInput").ap() for n, a in arrays.items()]
    args.append(nc.dram_tensor("out_0", (1, T, D), mybir.dt.float32, kind="ExternalOutput").ap())
    decoder(nc, *args)
    r = run_bass_kernel_spmd(nc, [arrays], core_ids=[0])
    return r.results[0]["out_0"]
```
